# Optimizing a Trainium2 kernel written in Bass

```python
import jax, jax.numpy as jnp
from jax import lax
import numpy as np

D_MODEL = 1024
BATCH = 1
SEQ = 256
DEPTH = 2

N_MIXERS = 2
N_RET_LAYERS = (DEPTH + 1) // 2
N_MLA_LAYERS = DEPTH // 2

ROPE_BASE = 10000.0
NORM_EPS = 1e-6

RET_HEADS = 4
RET_QK_DIM = D_MODEL // RET_HEADS
RET_V_DIM = 2 * RET_QK_DIM
RET_WIDTH = RET_HEADS * RET_V_DIM
RET_CHUNK = 128

MLA_HEADS = 16
MLA_NOPE = 128
MLA_ROPE = 64
MLA_V = 128
Q_LORA = 3 * D_MODEL // 4
KV_LORA = D_MODEL // 4
MLA_WIDTH = MLA_HEADS * MLA_V
Q_BLOCK = 128

PLE_DIM = 256


def rms_norm(x, g):
    xf = x.astype(jnp.float32)
    y = xf * lax.rsqrt(jnp.mean(xf * xf, axis=-1, keepdims=True) + NORM_EPS)
    return (y * g.astype(jnp.float32)).astype(x.dtype)

def rope(x, pos):
    half = x.shape[-1] // 2
    inv_freq = ROPE_BASE ** (-jnp.arange(half, dtype=jnp.float32) / half)
    ang = pos.astype(jnp.float32)[..., None] * inv_freq
    cos = jnp.cos(ang)[:, :, None, :]
    sin = jnp.sin(ang)[:, :, None, :]
    xf = x.astype(jnp.float32)
    x1, x2 = xf[..., :half], xf[..., half:]
    return jnp.concatenate([x1 * cos - x2 * sin, x2 * cos + x1 * sin], axis=-1).astype(x.dtype)

def retention_branch(h, pos, w_in, gn_g, w_out):
    B, S, _ = h.shape
    n_chunks = S // RET_CHUNK
    z = h @ w_in
    qk_w = RET_HEADS * RET_QK_DIM
    q = z[..., :qk_w].reshape(B, S, RET_HEADS, RET_QK_DIM)
    k = z[..., qk_w:2 * qk_w].reshape(B, S, RET_HEADS, RET_QK_DIM)
    v = z[..., 2 * qk_w:2 * qk_w + RET_WIDTH].reshape(B, S, RET_HEADS, RET_V_DIM)
    gate = z[..., 2 * qk_w + RET_WIDTH:]
    q = rope(q, pos)
    k = rope(k, pos) * (RET_QK_DIM ** -0.5)

    log_g = jnp.log(1.0 - 2.0 ** (-5.0 - jnp.arange(RET_HEADS, dtype=jnp.float32)))
    idx = jnp.arange(RET_CHUNK, dtype=jnp.float32)
    rel = idx[:, None] - idx[None, :]
    dmask = jnp.where(rel[None] >= 0, jnp.exp(jnp.maximum(rel, 0.0)[None] * log_g[:, None, None]), 0.0)
    q_decay = jnp.exp((idx + 1.0)[None, :] * log_g[:, None])
    k_decay = jnp.exp((RET_CHUNK - 1.0 - idx)[None, :] * log_g[:, None])
    c_decay = jnp.exp(RET_CHUNK * log_g)

    def to_chunks(t):
        return t.astype(jnp.float32).reshape(B, n_chunks, RET_CHUNK, RET_HEADS, t.shape[-1]).transpose(1, 0, 3, 2, 4)

    qc, kc, vc = to_chunks(q), to_chunks(k), to_chunks(v)

    def step(state, inp):
        qb, kb, vb = inp
        a = jnp.einsum('bhid,bhjd->bhij', qb, kb) * dmask
        o = jnp.einsum('bhij,bhjv->bhiv', a, vb) + jnp.einsum(
            'bhid,bhdv->bhiv', qb * q_decay[..., None], state)
        state = state * c_decay[:, None, None] + jnp.einsum(
            'bhjd,bhjv->bhdv', kb * k_decay[..., None], vb)
        return state, o

    s0 = jnp.zeros((B, RET_HEADS, RET_QK_DIM, RET_V_DIM), jnp.float32)
    _, o = lax.scan(step, s0, (qc, kc, vc))
    o = o.transpose(1, 0, 3, 2, 4).reshape(B, S, RET_HEADS, RET_V_DIM)
    o = o * lax.rsqrt(jnp.mean(o * o, axis=-1, keepdims=True) + NORM_EPS)
    o = (o.reshape(B, S, RET_WIDTH) * gn_g.astype(jnp.float32)).astype(h.dtype)
    return (jax.nn.silu(gate) * o) @ w_out

def mla_branch(h, pos, w_in, q_norm_g, kv_norm_g, w_uq, w_uk, w_uv, w_out):
    B, S, _ = h.shape
    n_blocks = S // Q_BLOCK
    z = h @ w_in
    o1, o2, o3 = Q_LORA, Q_LORA + KV_LORA, Q_LORA + KV_LORA + MLA_ROPE
    c_q = rms_norm(z[..., :o1], q_norm_g)
    c_kv = rms_norm(z[..., o1:o2], kv_norm_g)
    k_rope = rope(z[..., o2:o3][:, :, None, :], pos)[:, :, 0, :]
    gate = z[..., o3:]

    q = (c_q @ w_uq).reshape(B, S, MLA_HEADS, MLA_NOPE + MLA_ROPE)
    q_nope = q[..., :MLA_NOPE]
    q_rope = rope(q[..., MLA_NOPE:], pos)
    q_abs = jnp.einsum('bshd,chd->bshc', q_nope, w_uk)
    scale = (MLA_NOPE + MLA_ROPE) ** -0.5
    q_cat = jnp.concatenate([q_abs, q_rope], axis=-1) * scale
    k_cat = jnp.concatenate([c_kv, k_rope], axis=-1)
    q_blocks = q_cat.reshape(B, n_blocks, Q_BLOCK, MLA_HEADS, -1).transpose(1, 0, 2, 3, 4)
    key_idx = jnp.arange(S)
    neg = jnp.finfo(jnp.float32).min

    def attend(args):
        qb, bi = args
        s = jnp.einsum('bqhc,bkc->bhqk', qb, k_cat).astype(jnp.float32)
        q_idx = bi * Q_BLOCK + jnp.arange(Q_BLOCK)
        s = jnp.where(key_idx[None, :] <= q_idx[:, None], s, neg)
        pr = jax.nn.softmax(s, axis=-1).astype(c_kv.dtype)
        return jnp.einsum('bhqk,bkc->bqhc', pr, c_kv)

    o_lat = lax.map(attend, (q_blocks, jnp.arange(n_blocks)))
    o_lat = o_lat.transpose(1, 0, 2, 3, 4).reshape(B, S, MLA_HEADS, KV_LORA)
    o = jnp.einsum('bshc,chd->bshd', o_lat, w_uv).reshape(B, S, MLA_WIDTH)
    return (jax.nn.silu(gate) * o) @ w_out

def first_inputs(seed: int = 0) -> dict:
    key = jax.random.key(seed)
    ks = jax.random.split(key, 20)
    f32 = jnp.float32

    def w(k, shape, fan_in):
        return jax.random.normal(k, shape, f32) * (fan_in ** -0.5)

    def gain(k, shape):
        return 1.0 + 0.02 * jax.random.normal(k, shape, f32)

    ret_in_w = 2 * RET_HEADS * RET_QK_DIM + 2 * RET_WIDTH
    mla_in_w = Q_LORA + KV_LORA + MLA_ROPE + MLA_WIDTH
    offset = jax.random.randint(ks[2], (BATCH, 1), 0, 4096, dtype=jnp.int32)
    return {
        "x": jax.random.normal(ks[0], (BATCH, SEQ, D_MODEL), f32),
        "p": jax.random.normal(ks[1], (DEPTH, BATCH, SEQ, PLE_DIM), f32),
        "positions": offset + jnp.arange(SEQ, dtype=jnp.int32)[None, :],
        "pre_norm_g": gain(ks[3], (DEPTH, D_MODEL)),
        "post_norm_g": gain(ks[4], (DEPTH, D_MODEL)),
        "ret_w_in": w(ks[5], (N_RET_LAYERS, D_MODEL, ret_in_w), D_MODEL),
        "ret_gn_g": gain(ks[6], (N_RET_LAYERS, RET_WIDTH)),
        "ret_w_out": w(ks[7], (N_RET_LAYERS, RET_WIDTH, D_MODEL), RET_WIDTH),
        "mla_w_in": w(ks[8], (N_MLA_LAYERS, D_MODEL, mla_in_w), D_MODEL),
        "mla_q_norm_g": gain(ks[9], (N_MLA_LAYERS, Q_LORA)),
        "mla_kv_norm_g": gain(ks[10], (N_MLA_LAYERS, KV_LORA)),
        "mla_w_uq": w(ks[11], (N_MLA_LAYERS, Q_LORA, MLA_HEADS * (MLA_NOPE + MLA_ROPE)), Q_LORA),
        "mla_w_uk": w(ks[12], (N_MLA_LAYERS, KV_LORA, MLA_HEADS, MLA_NOPE), KV_LORA),
        "mla_w_uv": w(ks[13], (N_MLA_LAYERS, KV_LORA, MLA_HEADS, MLA_V), KV_LORA),
        "mla_w_out": w(ks[14], (N_MLA_LAYERS, MLA_WIDTH, D_MODEL), MLA_WIDTH),
        "ple_w_proj": w(ks[15], (DEPTH, PLE_DIM, D_MODEL), PLE_DIM),
        "ple_w_gate": w(ks[16], (DEPTH, D_MODEL, D_MODEL), D_MODEL),
    }

def first_block(x, p, positions, pre_norm_g, post_norm_g, ret_w_in, ret_gn_g, ret_w_out,
              mla_w_in, mla_q_norm_g, mla_kv_norm_g, mla_w_uq, mla_w_uk, mla_w_uv, mla_w_out,
              ple_w_proj, ple_w_gate):
    for i in range(DEPTH):
        h = rms_norm(x, pre_norm_g[i])
        j = i // N_MIXERS
        if i % N_MIXERS == 0:
            y = retention_branch(h, positions, ret_w_in[j], ret_gn_g[j], ret_w_out[j])
        else:
            y = mla_branch(h, positions, mla_w_in[j], mla_q_norm_g[j], mla_kv_norm_g[j],
                           mla_w_uq[j], mla_w_uk[j], mla_w_uv[j], mla_w_out[j])
        x = x + rms_norm(y, post_norm_g[i])
        x = x + (p[i] @ ple_w_proj[i]) * jax.nn.sigmoid(x @ ple_w_gate[i])
    return x


DEPTH_2 = 1

CONV_CH = D_MODEL // 2
CONV_K = 31
CONV_GROUPS = 8
POOL_CH = D_MODEL // 2
POOL_WINDOWS = (2, 4, 8, 16)
N_POOL_GROUPS = len(POOL_WINDOWS)
POOL_GROUP_CH = POOL_CH // N_POOL_GROUPS
POOL_GROUP_OUT = D_MODEL // N_POOL_GROUPS
N_BRANCH = 2
COL_A_VAL = CONV_CH
COL_A_GATE = 2 * CONV_CH
COL_POOL = 2 * CONV_CH + POOL_CH
COL_GATE_A = COL_POOL + D_MODEL
IN_COLS = COL_POOL + N_BRANCH * D_MODEL
D_FF = ((8 * D_MODEL // 3 + 127) // 128) * 128
FFN_K = 3
ALPHA = (2.0 * DEPTH_2) ** 0.25
BETA = (8.0 * DEPTH_2) ** -0.25
LN_EPS = 1e-5
N_MOD = 6


def layer_norm(x, g=None, b=None):
    xf = x.astype(jnp.float32)
    mu = jnp.mean(xf, axis=-1, keepdims=True)
    var = jnp.mean(jnp.square(xf - mu), axis=-1, keepdims=True)
    y = (xf - mu) * lax.rsqrt(var + LN_EPS)
    if g is not None:
        y = y * g.astype(jnp.float32) + b.astype(jnp.float32)
    return y.astype(x.dtype)

def causal_dwconv(x, w, b):
    k, ch = w.shape
    y = lax.conv_general_dilated(
        x, w[:, None, :].astype(x.dtype), window_strides=(1,),
        padding=[(k - 1, 0)], dimension_numbers=("NWC", "WIO", "NWC"),
        feature_group_count=ch)
    return y + b.astype(x.dtype)

def causal_multiscale_pool(u):
    bsz, s, _ = u.shape
    ug = u.reshape(bsz, s, N_POOL_GROUPS, POOL_GROUP_CH).astype(jnp.float32)
    cs = jnp.cumsum(ug, axis=1)
    pos = jnp.arange(s)
    outs = []
    for gi, w in enumerate(POOL_WINDOWS):
        c_g = cs[:, :, gi]
        lag = jnp.pad(c_g, ((0, 0), (w, 0), (0, 0)))[:, :s]
        cnt = jnp.minimum(pos + 1, w).astype(jnp.float32)[None, :, None]
        outs.append((c_g - lag) / cnt)
    pooled = jnp.stack(outs, axis=2)
    return (pooled - ug).astype(u.dtype)

def second_inputs(seed: int = 0) -> dict:
    key = jax.random.key(seed)
    ks = jax.random.split(key, 24)
    f32 = jnp.float32
    L = DEPTH_2

    def nrm(k, shape, scale):
        return jax.random.normal(k, shape, f32) * scale

    def gain(k, shape):
        return 1.0 + 0.05 * jax.random.normal(k, shape, f32)

    return {
        "x": jax.random.normal(ks[0], (BATCH, SEQ, D_MODEL), f32),
        "c": jax.random.normal(ks[1], (BATCH, D_MODEL), f32),
        "w_ada": nrm(ks[2], (L, D_MODEL, N_MOD * D_MODEL), 0.5 * D_MODEL ** -0.5),
        "b_ada": nrm(ks[3], (L, N_MOD * D_MODEL), 0.02),
        "w_in": nrm(ks[4], (L, D_MODEL, IN_COLS), D_MODEL ** -0.5),
        "w_dw_a": nrm(ks[5], (L, CONV_K, CONV_CH), CONV_K ** -0.5),
        "b_dw_a": nrm(ks[6], (L, CONV_CH), 0.02),
        "ln_a_g": gain(ks[7], (L, CONV_CH)),
        "ln_a_b": nrm(ks[8], (L, CONV_CH), 0.02),
        "w_pw_a": nrm(ks[9], (L, CONV_CH, D_MODEL), BETA * CONV_CH ** -0.5),
        "w_pool": nrm(ks[10], (L, N_POOL_GROUPS, POOL_GROUP_CH, POOL_GROUP_OUT), BETA * POOL_GROUP_CH ** -0.5),
        "pool_scale": gain(ks[11], (L, D_MODEL)),
        "w_out": nrm(ks[12], (L, D_MODEL, D_MODEL), BETA * D_MODEL ** -0.5),
        "ln1_g": gain(ks[13], (L, D_MODEL)),
        "ln1_b": nrm(ks[14], (L, D_MODEL), 0.02),
        "w_up": nrm(ks[15], (L, D_MODEL, 2 * D_FF), BETA * D_MODEL ** -0.5),
        "w_dw_f": nrm(ks[16], (L, FFN_K, 2 * D_FF), FFN_K ** -0.5),
        "b_dw_f": nrm(ks[17], (L, 2 * D_FF), 0.02),
        "w_down": nrm(ks[18], (L, D_FF, D_MODEL), BETA * D_FF ** -0.5),
        "ln2_g": gain(ks[19], (L, D_MODEL)),
        "ln2_b": nrm(ks[20], (L, D_MODEL), 0.02),
    }

def second_block(x, c, w_ada, b_ada, w_in, w_dw_a, b_dw_a, ln_a_g, ln_a_b, w_pw_a,
              w_pool, pool_scale, w_out, ln1_g, ln1_b, w_up, w_dw_f, b_dw_f,
              w_down, ln2_g, ln2_b):
    bsz, s, _ = x.shape
    for l in range(DEPTH_2):
        mod = jax.nn.silu(c) @ w_ada[l] + b_ada[l]
        sh1, sc1, g1, sh2, sc2, g2 = jnp.split(mod, N_MOD, axis=-1)

        h = layer_norm(x) * (1.0 + sc1[:, None]) + sh1[:, None]
        proj = h @ w_in[l]
        a_val, a_gate, u_pool, gate_a, gate_b = jnp.split(
            proj, [COL_A_VAL, COL_A_GATE, COL_POOL, COL_GATE_A], axis=-1)

        ya = a_val * jax.nn.sigmoid(a_gate)
        ya = causal_dwconv(ya, w_dw_a[l], b_dw_a[l])
        ya = jax.nn.silu(layer_norm(ya, ln_a_g[l], ln_a_b[l]))
        ya = ya @ w_pw_a[l]

        pooled = causal_multiscale_pool(u_pool)
        yb = jnp.einsum("bsgc,gcd->bsgd", pooled, w_pool[l]).reshape(bsz, s, D_MODEL)
        yb = yb * pool_scale[l]

        merged = jax.nn.sigmoid(gate_a) * ya + jax.nn.sigmoid(gate_b) * yb
        mix = merged @ w_out[l]
        x = layer_norm(ALPHA * x + g1[:, None] * mix, ln1_g[l], ln1_b[l])

        h = layer_norm(x) * (1.0 + sc2[:, None]) + sh2[:, None]
        up = causal_dwconv(h @ w_up[l], w_dw_f[l], b_dw_f[l])
        v, gt = jnp.split(up, 2, axis=-1)
        f = (jax.nn.gelu(gt) * v) @ w_down[l]
        x = layer_norm(ALPHA * x + g2[:, None] * f, ln2_g[l], ln2_b[l])
    return x


def setup_inputs(seed=0):
    out = dict(first_inputs(seed))
    for name, value in second_inputs(seed + 1).items():
        if name != "x":
            out[name + "_2"] = value
    return out


def reference(
    x, p, positions, pre_norm_g, post_norm_g, ret_w_in, ret_gn_g, ret_w_out, mla_w_in,
    mla_q_norm_g, mla_kv_norm_g, mla_w_uq, mla_w_uk, mla_w_uv, mla_w_out, ple_w_proj,
    ple_w_gate, c_2, w_ada_2, b_ada_2, w_in_2, w_dw_a_2, b_dw_a_2, ln_a_g_2, ln_a_b_2, w_pw_a_2,
    w_pool_2, pool_scale_2, w_out_2, ln1_g_2, ln1_b_2, w_up_2, w_dw_f_2, b_dw_f_2, w_down_2,
    ln2_g_2, ln2_b_2,
):
    x = first_block(
        x, p, positions, pre_norm_g, post_norm_g, ret_w_in, ret_gn_g, ret_w_out, mla_w_in,
        mla_q_norm_g, mla_kv_norm_g, mla_w_uq, mla_w_uk, mla_w_uv, mla_w_out, ple_w_proj,
        ple_w_gate,
    )
    return second_block(
        x, c_2, w_ada_2, b_ada_2, w_in_2, w_dw_a_2, b_dw_a_2, ln_a_g_2, ln_a_b_2, w_pw_a_2,
        w_pool_2, pool_scale_2, w_out_2, ln1_g_2, ln1_b_2, w_up_2, w_dw_f_2, b_dw_f_2, w_down_2,
        ln2_g_2, ln2_b_2,
    )


_drawn_inputs = setup_inputs


def setup_inputs(seed=0):
    import zlib

    import numpy as np

    out = dict(_drawn_inputs(seed))
    spreads = {}
    factors = {'post_norm_g': 2.781,
     'ret_gn_g': 3.234,
     'mla_q_norm_g': 5.723,
     'mla_kv_norm_g': 3.746,
     'b_ada_2': 8.0,
     'w_dw_a_2': 3.903,
     'b_dw_a_2': 8.0,
     'ln_a_g_2': 35.102,
     'ln_a_b_2': 64.0,
     'w_pw_a_2': 3.651,
     'pool_scale_2': 64.0,
     'ln1_b_2': 2.856,
     'b_dw_f_2': 27.409,
     'ln2_b_2': 2.832}
    for name, (base, spread) in spreads.items():
        noise = np.random.default_rng([zlib.crc32(name.encode()), seed]).standard_normal(out[name].shape)
        drawn = base * np.exp(spread * noise) if base else spread * noise
        out[name] = __import__('jax').numpy.asarray(drawn.astype(out[name].dtype))
    for name, factor in factors.items():
        out[name] = (out[name] * factor).astype(out[name].dtype)
    return out
```

```python
from contextlib import ExitStack

import numpy as np

import concourse.bass as bass
from concourse import mybir

F32 = mybir.dt.float32
F32R = mybir.dt.float32r
I32 = mybir.dt.int32
ALU = mybir.AluOpType
AX_X = mybir.AxisListType.X
ACT = mybir.ActivationFunctionType

P = 128
T = 256
D = 1024
DT = D // P
RING = 4
AHEAD = 3
RET_HEADS, RET_V = 4, 512
MLA_HEADS, MLA_NOPE, MLA_ROPE = 16, 128, 64
Q_TILES, KV_TILES = 6, 2
CONV_K, CONV_TILES = 31, 4
WINDOWS = (2, 4, 8, 16)
FF_TILES = 22
SCALE = (MLA_NOPE + MLA_ROPE) ** -0.5
ALPHA = 2.0 ** 0.25
RMS_EPS, LN_EPS = 1e-6, 1e-5
TWO_PI = 2.0 * np.pi
NEG = -3.0e38

COLS = {}
_n = 0
for _name, _w in (("pre0", 8), ("pre1", 8), ("post0", 8), ("post1", 8), ("gn", 16), ("qn", 6), ("kvn", 2),
                  ("bada", 48), ("c", 8), ("dwa", CONV_TILES * CONV_K), ("bdwa", 4), ("lnag", 4), ("lnab", 4),
                  ("ps", 8), ("ln1g", 8), ("ln1b", 8), ("dwf", 44 * 3), ("bdwf", 44), ("ln2g", 8), ("ln2b", 8),
                  ("invf_ret", 1), ("invf_mla", 1), ("rms_eps", 1), ("ln_eps", 1)):
    COLS[_name] = _n
    _n += _w
NCOLS = _n

B_HEAD = 0
B_RO = B_HEAD + 12 * RET_HEADS
B_PJ0 = B_RO + 16
B_PG0 = B_PJ0 + 2
B_MIN = B_PG0 + 8
B_MG = B_MIN + 10
B_GRP = B_MG + 16
B_MO = B_GRP + 32
B_PJ1 = B_MO + 16
B_PG1 = B_PJ1 + 2
B_WA = B_PG1 + 8
B_WP = B_WA + 8
B_WG = B_WP + 4
B_POOL = B_WG + 16
B_PW = B_POOL + 1
B_WO = B_PW + 4
B_UP = B_WO + 8
B_DN = B_UP + 2 * FF_TILES
B_END = B_DN + 4 * DT
DN_TILES = (6, 6, 5, 5)

A_HEAD = 0
A_RO = A_HEAD + 2 * RET_HEADS
A_PJ0 = A_RO + 8
A_PG0 = A_PJ0 + 4
A_MIN = A_PG0 + 4
A_MG = A_MIN + 4
A_GRP = A_MG + 8
A_MO = A_GRP + 16
A_PJ1 = A_MO + 8
A_PG1 = A_PJ1 + 4
A_WP = A_PG1 + 4
A_WG = A_WP + 2
A_UP = A_WG + 8
V_HEAD = 0
V_KR = V_HEAD + 2 * RET_HEADS
V_WA = V_KR + 2
V_POOL = V_WA + 4
V_PW = V_POOL + 4
V_WO = V_PW + 4
V_DN = V_WO + 4

S_PRE0, S_POST0, S_PRE1, S_Q, S_KV, S_POST1, S_LNA, S_CONV, S_LN1, S_LNB, S_LN2 = range(11)
SQ_INCS = (4, 8, 4, 3, 1, 8, 4, 2, 4, 4, 4)


def sq_before(s):
    return sum(SQ_INCS[:s])


LN_PAIRS = (4, 2, 4, 4, 4)
LN_INDEX = {S_LNA: 0, S_CONV: 1, S_LN1: 2, S_LNB: 3, S_LN2: 4}

H_RET, H_PLE0, H_MLA, H_PLE1, H_CONV, H_MERGED, H_FF = range(7)

X_POST0, X_PLE0, X_POST1, X_PLE1, X_DONE = 0, 8, 12, 20, 24
AFF = (0, 8, 12, 20, 28)
AFF_END = 36
T_BEFORE = (0, 4, 8, 12, 15, 16, 20, 24, 26, 30, 34)
HH_BEFORE = (0, 8, 12, 20, 24, 28, 32)
TURN = (6.28125, float(np.float32(0.0019350051879882812)), 2.0 * np.pi - 6.28125 - 0.0019350051879882812)
ROUND = 1.5 * 2.0 ** 23
PI_IN = 3.1415925


def program(nc, x_in, p_in, pos_in, cols_in, mask_in, tri_in, cnt_in, ident_in, ada_in, w, out):
    ctx = ExitStack()
    with ctx:
        def sb(name, shape, dt=F32):
            return ctx.enter_context(nc.sbuf_tensor(name, shape, dt))

        def sem(name):
            return ctx.enter_context(nc.semaphore(name))

        raw = sb("raw", [P, RING, 1024])
        whi = sb("whi", [P, RING, 1024], F32R)
        wlo = sb("wlo", [P, RING, 1024], F32R)
        ada_raw = sb("ada_raw", [P, 2, 1024])
        ada_acc = sb("ada_acc", [P, 2, 1024])
        X = sb("X", [P, DT, T])
        Hh = sb("Hh", [P, DT, T], F32R)
        Hl = sb("Hl", [P, DT, T], F32R)
        Yh = sb("Yh", [P, FF_TILES, T], F32R)
        Yl = sb("Yl", [P, FF_TILES, T], F32R)
        Sh = sb("Sh", [P, 4, T], F32R)
        Sl = sb("Sl", [P, 4, T], F32R)
        Z = sb("Z", [P, DT, T])
        G = sb("G", [P, 16, T])
        praw = sb("praw", [P, 2, T])
        WK = sb("WK", [P, 20, T])
        TAB = sb("TAB", [P, 4, T])
        maskd = sb("maskd", [P, RET_HEADS, T])
        tri = sb("tri", [P, 3 * P])
        cnt = sb("cnt", [P, 4, 16])
        cols = sb("cols", [P, NCOLS])
        ident = sb("ident", [P, P])
        ones = sb("ones", [P, P])
        mod = sb("mod", [P, 48])
        siluc = sb("siluc", [P, 8])
        root = sb("root", [P, T])
        rstd = sb("rstd", [P, T])
        mean = sb("mean", [P, T])
        SGT = sb("SGT", [P, 2, 512])
        small = sb("small", [P, 2, 8])
        prime = sb("prime", [P, 8])

        PP = WK[:, 0:8, :]
        SQ = WK[:, 8:16, :]
        Q, K = WK[:, 0:2, :], WK[:, 2:4, :]
        V = WK[:, 4:8, :].rearrange("p a t -> p (a t)").rearrange("p (t v) -> p t v", t=2)
        AT = WK[:, 16:18, :].rearrange("p a t -> p (a t)")
        TA = WK[:, 12:14, :]
        TB = WK[:, 14:16, :]
        SG = G[:, 0:4, :]
        YF = G[:, 4:8, :]
        KR = WK[:, 18:20, :]
        QN, KN = WK[:, 0:4, :], WK[:, 8:12, :]
        QR = WK[:, 12:14, :]
        SM = WK[:, 14:17, :].rearrange("p a t -> p (a t)").rearrange("p (s n) -> p s n", s=2)
        PT = Z[:, 0:3, :].rearrange("p a t -> p (a t)").rearrange("p (s n) -> p s n", s=2)
        YG = Z[:, 4:8, :]
        TC = SGT
        CI = WK[:, 0:5, :].rearrange("p a t -> p (a t)")[:, 0:4 * 286].rearrange("p (c n) -> p c n", c=4)
        CO = WK[:, 16:20, :]
        U = WK[:, 5:10, :].rearrange("p a t -> p (a t)")[:, 0:4 * 272].rearrange("p (c n) -> p c n", c=4)
        W1 = WK[:, 10:13, :].rearrange("p a t -> p (a t)")[:, 0:2 * 272].rearrange("p (c n) -> p c n", c=2)
        PO = Z[:, 4:8, :]
        UPAD = WK[:, 0:5, :].rearrange("p a t -> p (a t)")[:, 0:4 * 258].rearrange("p (c n) -> p c n", c=4)
        CV = WK[:, 8:12, :]
        GG = WK[:, 12:14, :]
        FF = WK[:, 14:16, :]
        posi, posf = WK[:, 0, :].bitcast(I32), WK[:, 1, :]
        rk, rt = WK[:, 16:20, :], WK[:, 4:8, :]

        bank = [ctx.enter_context(nc.psum_tensor(f"bank{i}", [P, 512], F32)) for i in range(8)]
        GA, GD = bank[0:2], bank[2:4]
        M0, M1, M2, M3 = bank[4:8]

        raw_loaded = [sem(f"raw_loaded{s}") for s in range(RING)]
        lo_done, hi_done, pe_done = sem("lo_done"), sem("hi_done"), sem("pe_done")
        act_free, dve_free = sem("act_free"), sem("dve_free")
        ada_loaded = [sem(f"ada_loaded{s}") for s in range(2)]
        ada_used, mod_psum, mod_done = sem("ada_used"), sem("mod_psum"), sem("mod_done")
        ada_zero = sem("ada_zero")
        in_cols, in_x, in_pos, in_const, in_p = sem("in_cols"), sem("in_x"), sem("in_pos"), sem("in_const"), sem("in_p")
        const_ready = sem("const_ready")
        trig_step, trig_arg, trig_ready = sem("trig_step"), sem("trig_arg"), sem("trig_ready")
        silu_c = sem("silu_c")
        sq_ready, stat_ready, root_done, rstd_ready = sem("sq_ready"), sem("stat_ready"), sem("root_done"), sem("rstd_ready")
        mean_psum, mean_ready, centred = sem("mean_psum"), sem("mean_ready"), sem("centred")
        t_ready, hh_ready, h_ready = sem("t_ready"), sem("hh_ready"), sem("h_ready")
        rope_tmp, rope_ready = sem("rope_tmp"), sem("rope_ready")
        v_ready, at_ready, atm_ready = sem("v_ready"), sem("at_ready"), sem("atm_ready")
        o_ready, o_free = sem("o_ready"), sem("o_free")
        gsq, gstat, groot, grs = sem("gsq"), sem("gstat"), sem("groot"), sem("grs")
        yf_ready, yh_ready, y_ready = sem("yf_ready"), sem("yh_ready"), sem("y_ready")
        ph_ready, p_ready, rope_read, mod_one, ci_pad = (sem("ph_ready"), sem("p_ready"), sem("rope_read"), sem("mod_one"),
                                                        sem("ci_pad"))
        x_ready, gate_t = sem("x_ready"), sem("gate_t")
        sgt_ready = sem("sgt_ready")
        cqh_ready, cq_ready = sem("cqh_ready"), sem("cq_ready")
        mv_ready, qr_ready = sem("mv_ready"), sem("qr_ready")
        s_psum, s_masked, s_bias, s_exp, s_inv, s_prob = (sem("s_psum"), sem("s_masked"), sem("s_bias"), sem("s_exp"),
                                                        sem("s_inv"), sem("s_prob"))
        s_max = sem("s_max")
        t_psum, pt_ready, mo_psum, mo_gated = sem("t_psum"), sem("pt_ready"), sem("mo_psum"), sem("mo_gated")
        pool_step, pooled, pooled_hi, pooled_ready = sem("pool_step"), sem("pooled"), sem("pooled_hi"), sem("pooled_ready")
        conv_step, act_conv, convh_ready, conv_ready, aff = (sem("conv_step"), sem("act_conv"), sem("convh_ready"),
                                                             sem("conv_ready"), sem("aff"))
        merged_t, xs_ready, pads = sem("merged_t"), sem("xs_ready"), sem("pads")
        cv0, cv_step, gg_ready = sem("cv0"), sem("cv_step"), sem("gg_ready")
        f_ready, fh_ready, fl_ready = sem("f_ready"), sem("fh_ready"), sem("fl_ready")
        stored = sem("stored")

        def col(name, t=0, n=1):
            return cols[:, COLS[name] + t:COLS[name] + t + n]

        def dcol(name, t):
            return cols[:, bass.ds(t + COLS[name], 1)]

        def pair(a, t):
            return a[:, 2 * t:2 * t + 2, :]

        def wide(b):
            return b[:].rearrange("p (a t) -> p a t", a=2)

        def over(a, n):
            return a.unsqueeze(1).to_broadcast([P, n, T])

        def f32(a):
            return a.bitcast(F32)

        block = ctx.enter_context(nc.Block())

        def finish(sp):
            for t in range(4):
                sp.wait_ge(aff, AFF_END - 8 + 2 * t + 2)
                sp.dma_start(out[:, 2 * t:2 * t + 2, :], pair(X, t)).then_inc(stored, 16)
            sp.wait_ge(stored, 16 * 4)

        @block.sync
        def _(sp):
            def load(base, src, n, per=0, i=0):
                s = base % RING
                sp.wait_ge(lo_done, base + 1 + per * i)
                sp.dma_start(raw[:, s, 0:n], src).then_inc(raw_loaded[s], 16)

            def load_loop(base, name, count, per):
                blocks, n = w[name], w[name].shape[2]
                with sp.Fori(0, count) as i:
                    for j in range(per):
                        load(base + j, blocks[bass.ds(per * i + j, 1)].rearrange("b p n -> p (b n)"), n, per, i)

            def load_all(base, name):
                blocks, n = w[name], w[name].shape[2]
                for j in range(blocks.shape[0]):
                    load(base + j, blocks[j], n)

            sp.dma_start(cols[:], cols_in).then_inc(in_cols, 16)
            sp.dma_start(X[:], x_in).then_inc(in_x, 16)
            sp.dma_start(posi, pos_in.partition_broadcast(P)).then_inc(in_pos, 16)
            sp.dma_start(maskd[:], mask_in).then_inc(in_const, 16)
            sp.dma_start(tri[:], tri_in).then_inc(in_const, 16)
            sp.dma_start(cnt[:], cnt_in).then_inc(in_const, 16)
            sp.dma_start(ident[:], ident_in).then_inc(in_const, 16)
            sp.dma_start(praw[:], p_in[0]).then_inc(in_p, 16)
            load_loop(B_HEAD, "head", RET_HEADS, 12)
            load_loop(B_RO, "ret_out", 4, 4)
            load_all(B_PJ0, "proj0")
            load_loop(B_PG0, "ple_gate0", 2, 4)
            sp.wait_ge(p_ready, 1)
            sp.dma_start(praw[:], p_in[1]).then_inc(in_p, 16)
            load_loop(B_MIN, "mla_qkv", 2, 4)
            for j in range(2):
                load(B_MIN + 8 + j, w["mla_kr"][j], 1024)
            load_loop(B_MG, "mla_gate", 4, 4)
            with sp.Fori(0, 4) as i:
                load(B_GRP, w["uk"][bass.ds(i, 1)].rearrange("b p n -> p (b n)"), 1024, 8, i)
                load(B_GRP + 1, w["uv"][bass.ds(i, 1)].rearrange("b p n -> p (b n)"), 1024, 8, i)
                for j in range(6):
                    load(B_GRP + 2 + j, w["uq"][bass.ds(6 * i + j, 1)].rearrange("b p n -> p (b n)"), 768, 8, i)
            load_loop(B_MO, "mla_out", 4, 4)
            load_all(B_PJ1, "proj1")
            load_loop(B_PG1, "ple_gate1", 2, 4)
            load_loop(B_WA, "conv_in", 2, 4)
            load_all(B_WP, "pool_in")
            load_loop(B_WG, "gates", 4, 4)
            load_all(B_POOL, "pool_w")
            load_all(B_PW, "pw")
            load_loop(B_WO, "mix", 2, 4)
            load_loop(B_UP, "up", 11, 4)
            with sp.Fori(0, 4) as i:
                for j in range(8):
                    n = DN_TILES[j % 4] * P
                    load(B_DN + j, w["down"][bass.ds(8 * i + j, 1)].rearrange("b p n -> p (b n)")[:, 0:n], n, 8, i)
            finish(sp)

        @block.tensor
        def _(pe):
            mm = nc.tensor.matmul

            def products(base, parts, per=0, i=0, before=()):
                s = base % RING
                pe.wait_ge(lo_done, base + RING + 1 + per * i)
                for n, (t, ah, al, o, start, stop) in enumerate(parts):
                    if n < len(before) and before[n]:
                        pe.wait_ge(*before[n])
                    c = slice(t * P, t * P + P)
                    mm(o, whi[:, s, c], ah, start=start, stop=False)
                    mm(o, whi[:, s, c], al, start=False, stop=False)
                    last = mm(o, wlo[:, s, c], ah, start=False, stop=stop)
                last.then_inc(pe_done, 1)

            def strip(base, o, ah, al, per=0, i=0, before=()):
                products(base, [(k, ah[:, k, :], al[:, k, :], o, k == 0, k == 7) for k in range(8)], per, i, before)

            def free_a(k, per=0, i=0):
                pe.wait_ge(act_free, k + 1 + per * i)
                return GA[k % 2]

            def free_d(k, per=0, i=0):
                pe.wait_ge(dve_free, k + 1 + per * i)
                return GD[k % 2]

            def halves(b):
                return b[:, 0:T], b[:, T:2 * T]

            def h_waits(v):
                return [(h_ready, 4 * v + k // 2 + 1) if k % 2 == 0 else None for k in range(8)]

            def stats(s, n, b=None, tiles=None):
                b = M3 if b is None else b
                if s > 0:
                    pe.wait_ge(root_done, s)
                pe.wait_ge(sq_ready, sq_before(s + 1))
                for k in range(n) if tiles is None else tiles:
                    last = mm(b[:, 0:T], ones[:], SQ[:, k, :], start=(k == (tiles or [0])[0]),
                              stop=(k == (tiles[-1] if tiles else n - 1)))
                last.then_inc(stat_ready, 1)

            def mean_sum(s, src, n):
                pe.wait_ge(root_done, s)
                for k in range(n):
                    last = mm(M3[:, 0:T], ones[:], src[:, k, :], start=(k == 0), stop=(k == n - 1))
                last.then_inc(mean_psum, 1)

            def mod_columns(g, n):
                pe.wait_ge(ada_used, 2 + 8 * (g + n))
                if g > 0:
                    pe.wait_ge(mod_done, max(g - 1, 1))
                for a in range(n):
                    for t in range(8):
                        last = mm(M2[:, 8 * a + t:8 * a + t + 1], ada_acc[:, a, t * P:t * P + P], ones[:, 0:1],
                                  start=True, stop=True)
                last.then_inc(mod_psum, 1)

            def out_product(b0, a0, y0):
                with pe.Fori(0, 4) as i:
                    for t in range(2):
                        o = free_a(a0 + t, 2, i)[:, 0:T]
                        for c in range(2):
                            parts = [(k, Yh[:, 8 * c + k, :], Yl[:, 8 * c + k, :], o, c == 0 and k == 0, c == 1 and k == 7)
                                     for k in range(8)]
                            products(b0 + 2 * t + c, parts, 4, i, [(y_ready, y0 + 2 * c + 2)])

            def per_layer(s, bp, ap, bg, ag, v, layer):
                for c in range(2):
                    parts = []
                    for n in range(4):
                        o = GA[(ap + 2 * c + n // 2) % 2][:, T * (n % 2):T * (n % 2) + T]
                        parts += [(2 * n + k, Sh[:, k, :], Sl[:, k, :], o, k == 0, k == 1) for k in range(2)]
                    if c == 0:
                        pe.wait_ge(p_ready, layer + 1)
                    pe.wait_ge(act_free, ap + 2 * c + 1)
                    products(bp + c, parts, before=[None] * 4 + [(act_free, ap + 2 * c + 2)])
                    if c == 0:
                        stats(s, 8)
                with pe.Fori(0, 2) as i:
                    for j in range(4):
                        if j % 2 == 0:
                            b = free_a(ag + j // 2, 2, i)
                        strip(bg + j, halves(b)[j % 2], Hh, Hl, 4, i, h_waits(v) if j == 0 else ())

            def strips_a(base, a, count, v=None):
                with pe.Fori(0, count) as i:
                    for j in range(4):
                        if j % 2 == 0:
                            b = free_a(a + j // 2, 2, i)
                        strip(base + j, halves(b)[j % 2], Hh, Hl, 4, i, h_waits(v) if v is not None and j == 0 else ())

            def strips_d(base, d, count, v):
                with pe.Fori(0, count) as i:
                    for j in range(4):
                        if j % 2 == 0:
                            b = free_d(d + j // 2, 2, i)
                        strip(base + j, halves(b)[j % 2], Hh, Hl, 4, i, h_waits(v) if j == 0 else ())

            pe.wait_ge(const_ready, 1)
            stats(S_PRE0, 8)

            with pe.Fori(0, RET_HEADS) as i:
                for j in range(4):
                    if j % 2 == 0:
                        b = free_d(V_HEAD + j // 2, 2, i)
                    strip(B_HEAD + j, halves(b)[j % 2], Hh, Hl, 12, i, h_waits(H_RET) if j == 0 else ())
                pe.wait_ge(groot, i + 1)
                for j in range(4):
                    base = B_HEAD + 4 + j
                    s = base % RING
                    pe.wait_ge(lo_done, base + RING + 1 + 12 * i)
                    for k in range(2):
                        kk = 2 * j + k
                        c = slice(512 * k, 512 * k + 512)
                        for t, o in ((0, M0), (1, M1)):
                            tt = slice(P * t, P * t + P)
                            mm(o[:], Hh[:, kk, tt], whi[:, s, c], start=(kk == 0), stop=False)
                            mm(o[:], Hh[:, kk, tt], wlo[:, s, c], start=False, stop=False)
                            last = mm(o[:], Hl[:, kk, tt], whi[:, s, c], start=False, stop=(kk == 7))
                    last.then_inc(pe_done, 1)
                pe.wait_ge(rope_ready, 4 * i + 4)
                pe.wait_ge(o_free, i + 1)
                for d in range(2):
                    mm(M2[:, 0:T], K[:, d, 0:P], Q[:, d, :], start=(d == 0), stop=(d == 1))
                for d in range(2):
                    last = mm(M2[:, T:T + P], K[:, d, P:T], Q[:, d, P:T], start=(d == 0), stop=(d == 1))
                last.then_inc(at_ready, 1)
                b = free_a(A_HEAD, 2, i)
                strip(B_HEAD + 8, halves(b)[0], Hh, Hl, 12, i)
                strip(B_HEAD + 9, halves(b)[1], Hh, Hl, 12, i)
                pe.wait_ge(v_ready, 2 * i + 2)
                pe.wait_ge(atm_ready, 2 * i + 2)
                for t in range(4):
                    o = (M3, M2)[t // 2][:, T * (t % 2):T * (t % 2) + T]
                    c = slice(P * t, P * t + P)
                    mm(o, V[:, 0, c], AT[:, 0:T], start=True, stop=False)
                    last = mm(o[:, P:T], V[:, 1, c], AT[:, T:T + P], start=False, stop=True)
                    if t % 2 == 1:
                        last.then_inc(o_ready, 1)
                b = free_a(A_HEAD + 1, 2, i)
                strip(B_HEAD + 10, halves(b)[0], Hh, Hl, 12, i)
                pe.wait_ge(gsq, 2 * i + 2)
                for t in range(4):
                    last = mm(M1[:, 0:T], ones[:], SQ[:, t, :], start=(t == 0), stop=(t == 3))
                last.then_inc(gstat, 1)
                strip(B_HEAD + 11, halves(b)[1], Hh, Hl, 12, i)
            pe.wait_ge(o_free, RET_HEADS + 1)
            mod_columns(0, 2)
            out_product(B_RO, A_RO, 0)
            mod_columns(2, 1)
            per_layer(S_POST0, B_PJ0, A_PJ0, B_PG0, A_PG0, H_PLE0, 0)

            stats(S_PRE1, 8)
            strips_a(B_MIN, A_MIN, 2, H_MLA)
            b = free_d(V_KR)
            strip(B_MIN + 8, halves(b)[0], Hh, Hl)
            stats(S_Q, 6, tiles=list(range(6)))
            pe.wait_ge(sq_ready, sq_before(S_KV + 1))
            pe.wait_ge(mod_done, 2)
            for k in (6, 7):
                last = mm(M2[:, 0:T], ones[:], SQ[:, k, :], start=(k == 6), stop=(k == 7))
            last.then_inc(stat_ready, 1)
            strip(B_MIN + 9, halves(b)[1], Hh, Hl)
            strips_a(B_MG, A_MG, 4)
            pe.wait_ge(root_done, S_KV + 1)
            mod_columns(3, 1)
            pe.wait_ge(mod_done, 3)
            pe.wait_ge(cq_ready, Q_TILES + KV_TILES)
            pe.wait_ge(dve_free, V_WA + 2)
            with pe.Fori(0, 4) as i:
                parts, before = [], []
                for h in range(4):
                    o = GA[h // 2][:, T * (h % 2):T * (h % 2) + T]
                    parts += [(2 * h + k, Sh[:, 2 + k, :], Sl[:, 2 + k, :], o, k == 0, k == 1) for k in range(2)]
                pe.wait_ge(act_free, A_GRP + 1 + 4 * i)
                products(B_GRP, parts, 8, i, [None] * 4 + [(act_free, A_GRP + 2 + 4 * i)])
                pe.wait_ge(mo_gated, 4 * i + 1)
                s = (B_GRP + 1) % RING
                pe.wait_ge(lo_done, B_GRP + 1 + RING + 1 + 8 * i)
                for k in range(2):
                    c = slice(512 * k, 512 * k + 512)
                    for t, o in ((0, M0), (1, M1)):
                        tt = slice(P * t, P * t + P)
                        mm(o[:], Sh[:, 2 + k, tt], whi[:, s, c], start=(k == 0), stop=False)
                        mm(o[:], Sh[:, 2 + k, tt], wlo[:, s, c], start=False, stop=False)
                        last = mm(o[:], Sl[:, 2 + k, tt], whi[:, s, c], start=False, stop=(k == 1))
                last.then_inc(pe_done, 1)

                def latent_strip(j, o):
                    products(B_GRP + j, [(k, Yh[:, 16 + k, :], Yl[:, 16 + k, :], o, k == 0, k == 5) for k in range(6)], 8, i)

                def scores(h):
                    if h >= 2:
                        pe.wait_ge(s_masked, 4 * i + h - 1)
                    r = slice(32 * h, 32 * h + 32)
                    for q0, n, o in ((0, P, GD[h % 2][:, 0:P]), (P, T, GD[h % 2][:, P:P + T])):
                        mm(o, QN[:, h, q0:q0 + P], KN[:, h, 0:n], start=True, stop=False)
                        mm(o, QR[r, 0, q0:q0 + P], KR[r, 0, 0:n], start=False, stop=False)
                        last = mm(o, QR[r, 1, q0:q0 + P], KR[r, 1, 0:n], start=False, stop=True)
                    last.then_inc(s_psum, 1)

                def turn(h):
                    pe.wait_ge(s_prob, 8 * i + 2 * h + 2)
                    if h >= 2:
                        pe.wait_ge(pt_ready, 4 * i + h - 1)
                    b = (M3, M1)[h % 2]
                    nc.tensor.transpose(b[:, 0:P], SM[:, h % 2, 0:P], ident[:])
                    nc.tensor.transpose(b[:, P:T], SM[:, h % 2, P:T], ident[:])
                    nc.tensor.transpose(b[:, T:T + P], SM[:, h % 2, T:T + P], ident[:]).then_inc(t_psum, 1)

                def values(h):
                    pe.wait_ge(pt_ready, 4 * i + h + 1)
                    if h >= 2:
                        pe.wait_ge(mo_gated, 4 * i + h)
                    o = (M2, M0)[h % 2][:, 0:T]
                    c = slice(P * h, P * h + P)
                    mm(o, V[:, 0, c], PT[:, h % 2, 0:T], start=True, stop=False)
                    mm(o[:, P:T], V[:, 1, c], PT[:, h % 2, T:T + P], start=False, stop=True).then_inc(mo_psum, 1)

                latent_strip(2, M2[:, 0:T])
                latent_strip(3, M2[:, T:2 * T])
                pe.wait_ge(act_free, A_GRP + 3 + 4 * i)
                latent_strip(4, GA[0][:, 0:T])
                latent_strip(5, GA[0][:, T:2 * T])
                pe.wait_ge(act_free, A_GRP + 4 + 4 * i)
                latent_strip(6, GA[1][:, 0:T])
                pe.wait_ge(qr_ready, 2 * i + 4)
                pe.wait_ge(act_free, A_GRP + 5 + 4 * i)
                scores(0)
                scores(1)
                latent_strip(7, GA[1][:, T:2 * T])
                turn(0)
                turn(1)
                pe.wait_ge(act_free, A_GRP + 6 + 4 * i)
                scores(2)
                pe.wait_ge(mv_ready, 2 * i + 2)
                values(0)
                scores(3)
                values(1)
                turn(2)
                turn(3)
                values(2)
                values(3)
            pe.wait_ge(mo_gated, 4 * 4 + 1)
            mod_columns(4, 1)
            out_product(B_MO, A_MO, 4)
            mod_columns(5, 1)
            per_layer(S_POST1, B_PJ1, A_PJ1, B_PG1, A_PG1, H_PLE1, 1)

            pe.wait_ge(x_ready, X_DONE)
            mean_sum(S_LNA, X, 8)
            stats(S_LNA, 8)
            strips_d(B_WA, V_WA, 2, H_CONV)
            strips_a(B_WP, A_WP, 1)
            strips_a(B_WG, A_WG, 4)
            pe.wait_ge(conv_step, CONV_K * CONV_TILES)
            mean_sum(S_CONV, CO, 4)
            pe.wait_ge(pooled_ready, 1)
            pe.wait_ge(dve_free, V_POOL + 2)
            products(B_POOL, [(n, Sh[:, n // 2, :], Sl[:, n // 2, :], halves(bank[2 + n // 2])[n % 2], True, True)
                              for n in range(8)])
            stats(S_CONV, 4)
            pe.wait_ge(conv_ready, 2)
            for j in range(4):
                b = free_d(V_PW + j)
                products(B_PW + j, [(4 * n + k, Yh[:, k, :], Yl[:, k, :], halves(b)[n], k == 0, k == 3)
                                    for n in range(2) for k in range(4)])
            strips_d(B_WO, V_WO, 2, H_MERGED)
            pe.wait_ge(dve_free, V_DN + 2)
            mean_sum(S_LN1, X, 8)
            stats(S_LN1, 8)
            pe.wait_ge(aff, AFF[3])
            mean_sum(S_LNB, X, 8)
            stats(S_LNB, 8)
            strips_a(B_UP, A_UP, 11, H_FF)
            with pe.Fori(0, 4) as i:
                for t in range(2):
                    o = free_d(V_DN + t, 2, i)[:, 0:T]
                    k0 = 0
                    for c, n in enumerate(DN_TILES):
                        parts = [(k, Yh[:, k0 + k, :], Yl[:, k0 + k, :], o, k0 + k == 0, k0 + k == FF_TILES - 1)
                                 for k in range(n)]
                        products(B_DN + 4 * t + c, parts, 8, i, [(fl_ready, k0 + n)])
                        k0 += n
            pe.wait_ge(dve_free, V_DN + 8 + 2)
            mean_sum(S_LN2, X, 8)
            stats(S_LN2, 8)

        @block.scalar
        def _(act):
            activation = nc.scalar.activation

            def split(base, n=1024, per=0, i=0):
                b = base + AHEAD
                if b >= B_END:
                    return
                s = b % RING
                act.wait_ge(raw_loaded[s], 16 * (b // RING) + 16 + 16 * (per // RING) * i)
                act.wait_ge(pe_done, b + 1 + per * i)
                activation(whi[:, s, 0:n], raw[:, s, 0:n], ACT.Copy).then_inc(hi_done, 1)

            def used(base, per=0, i=0):
                act.wait_ge(pe_done, base + RING + 1 + per * i)

            def load_ada(x, per, i):
                for n in range(2):
                    act.wait_ge(ada_used, x + n + 1 + per * i)
                    act.dma_start(ada_raw[:, n, :], ada_in[bass.ds(per * i + x + n, 1)].rearrange("b p n -> p (b n)"))\
                       .then_inc(ada_loaded[n], 16)

            def square_pairs(s, src, n, ready=None):
                if s > 0:
                    act.wait_ge(stat_ready, s)
                for p in range(n):
                    if ready is not None:
                        act.wait_ge(ready[0], ready[1] + p + 1)
                    activation(pair(SQ, p), pair(src, p), ACT.Square).then_inc(sq_ready, 1)

            def root_of(s, n, eps="rms_eps", b=None):
                if s > 0:
                    act.wait_ge(rstd_ready, s)
                act.wait_ge(stat_ready, s + 1)
                activation(root[:], (M3 if b is None else b)[:, 0:T], ACT.Sqrt, bias=col(eps), scale=1.0 / n)\
                    .then_inc(root_done, 1)

            def scaled_hi(src, dst, gain, t0, n, out_sem, base):
                for t in range(n):
                    if t % 2 == 0:
                        act.wait_ge(t_ready, base + t // 2 + 1)
                    activation(dst[:, t0 + t, :], src[:, t, :], ACT.Copy, scale=col(gain, t)).then_inc(out_sem, 1)

            def pairs_hi(src, ready, base, step):
                for p in range(4):
                    act.wait_ge(ready, base + step * (p + 1))
                    activation(pair(Hh, p), pair(src, p), ACT.Copy).then_inc(hh_ready, 1)

            def dyn(a, t, n):
                return a[:, bass.ds(t, n), :]

            def out_evac(b0, s, ada0):
                act.wait_ge(stat_ready, s)

                def tile_out(t, i):
                    used(b0 + 2 * t + 1, 4, i)
                    o = GA[t][:, 0:T].unsqueeze(1)
                    activation(dyn(SQ, 2 * i + t, 1), o, ACT.Square).then_inc(sq_ready, 1)
                    activation(dyn(Z, 2 * i + t, 1), o, ACT.Copy).then_inc(act_free, 1)

                with act.Fori(0, 4) as i:
                    for j in range(4):
                        split(b0 + j, 1024, 4, i)
                        if j == 0:
                            load_ada(ada0, 2, i)
                        if j == 2:
                            tile_out(0, i)
                    tile_out(1, i)

            def proj_evac(bp):
                for c in range(2):
                    split(bp + c)
                for c in range(2):
                    used(bp + c)
                    for f in (2 * c, 2 * c + 1):
                        activation(pair(PP, f), wide(GA[f % 2]), ACT.Copy).then_inc(act_free, 1)

            def ple_gate(bg, x0, squares):
                def gate(f, i):
                    act.wait_ge(x_ready, x0 + 2 * i)
                    used(bg + 2 * f + 1, 4, i)
                    activation(SGT[:, f, :], GA[f][:], ACT.Sigmoid).then_inc(act_free, 1)

                def square(f, i):
                    act.wait_ge(x_ready, x0 + 2 * i + f + 1)
                    activation(dyn(SQ, 4 * i + 2 * f, 2), dyn(X, 4 * i + 2 * f, 2), ACT.Square).then_inc(sq_ready, 1)

                with act.Fori(0, 2) as i:
                    for j in range(4):
                        split(bg + j, 1024, 4, i)
                        if j == 2:
                            gate(0, i)
                        if j == 3 and squares:
                            square(0, i)
                    gate(1, i)
                    if squares:
                        square(1, i)

            def p_hi(layer):
                act.wait_ge(in_p, 16 * layer + 16)
                activation(Sh[:, 0:2, :], praw[:], ACT.Copy).then_inc(ph_ready, 1)

            def evac(base, f, dst, func, per=0, i=0):
                used(base, per, i)
                activation(dst, wide(GA[f % 2]), func).then_inc(act_free, 1)

            act.wait_ge(in_x, 16)
            square_pairs(S_PRE0, X, 4)
            act.wait_ge(in_cols, 16)
            activation(siluc[:], col("c", 0, 8), ACT.Silu).then_inc(silu_c, 1)
            for b in range(AHEAD):
                split(b - AHEAD)
            root_of(S_PRE0, D)
            scaled_hi(Z, Hh, "pre0", 0, DT, hh_ready, T_BEFORE[S_PRE0])
            act.wait_ge(trig_arg, 1)
            activation(TAB[:], rt, ACT.Sin).then_inc(trig_ready, 1)
            p_hi(0)

            with act.Fori(0, RET_HEADS) as i:
                for j in range(12):
                    split(B_HEAD + j, 1024, 12, i)
                    if j in (0, 5):
                        load_ada(0 if j == 0 else 2, 4, i)
                    if j == 8:
                        used(B_HEAD + 7, 12, i)
                        activation(V[:, 0, :], M0[:], ACT.Copy).then_inc(v_ready, 1)
                        activation(V[:, 1, :], M1[:], ACT.Copy).then_inc(v_ready, 1)
                    if j == 10:
                        evac(B_HEAD + 9, 0, SG[:, 0:2, :], ACT.Silu, 12, i)
                        for f, b in ((0, M3), (1, M2)):
                            act.wait_ge(o_ready, 2 * i + f + 1)
                            activation(pair(SQ, f), wide(b), ACT.Square).then_inc(gsq, 1)
                    if j == 11:
                        act.wait_ge(gstat, i + 1)
                        activation(root[:], M1[:, 0:T], ACT.Sqrt, bias=col("rms_eps"), scale=1.0 / RET_V).then_inc(groot, 1)
                evac(B_HEAD + 11, 1, SG[:, 2:4, :], ACT.Silu, 12, i)
                act.wait_ge(yf_ready, i + 1)
                activation(dyn(Yh, 4 * i, 4), YF, ACT.Copy).then_inc(yh_ready, 1)
            out_evac(B_RO, S_POST0, 16)
            split(B_PJ0)
            root_of(S_POST0, D)
            split(B_PJ0 + 1)
            for c in range(2):
                for f in (2 * c, 2 * c + 1):
                    evac(B_PJ0 + c, f, pair(PP, f), ACT.Copy)
            pairs_hi(X, x_ready, X_POST0, 2)
            ple_gate(B_PG0, X_PLE0, True)

            root_of(S_PRE1, D)
            scaled_hi(Z, Hh, "pre1", 0, DT, hh_ready, T_BEFORE[S_PRE1])
            with act.Fori(0, 2) as i:
                for j in range(4):
                    split(B_MIN + j, 1024, 4, i)
                    if j == 2:
                        used(B_MIN + 1, 4, i)
                        activation(dyn(SQ, 4 * i, 2), wide(GA[0]), ACT.Square).then_inc(sq_ready, 1)
                        activation(dyn(Z, 4 * i, 2), wide(GA[0]), ACT.Copy).then_inc(act_free, 1)
                used(B_MIN + 3, 4, i)
                activation(dyn(SQ, 4 * i + 2, 2), wide(GA[1]), ACT.Square).then_inc(sq_ready, 1)
                activation(dyn(Z, 4 * i + 2, 2), wide(GA[1]), ACT.Copy).then_inc(act_free, 1)
            split(B_MIN + 8)
            split(B_MIN + 9)
            p_hi(1)
            root_of(S_Q, Q_TILES * P)
            root_of(S_KV, KV_TILES * P, b=M2)
            scaled_hi(Z, Yh, "qn", 16, Q_TILES, cqh_ready, T_BEFORE[S_Q])
            scaled_hi(Z[:, 6:8, :], Sh, "kvn", 2, KV_TILES, cqh_ready, T_BEFORE[S_KV])
            with act.Fori(0, 4) as i:
                for j in range(4):
                    split(B_MG + j, 1024, 4, i)
                    if j == 0:
                        load_ada(24, 2, i)
                    if j == 2:
                        evac(B_MG + 1, 0, dyn(G, 4 * i, 2), ACT.Silu, 4, i)
                evac(B_MG + 3, 1, dyn(G, 4 * i + 2, 2), ACT.Silu, 4, i)
            with act.Fori(0, 4) as i:
                def exps(h):
                    act.wait_ge(s_bias, 4 * i + h + 1)
                    s = h % 2
                    activation(SM[:, s, 0:P], SM[:, s, 0:P], ACT.Exp, bias=small[:, s, 2:3], scale=SCALE,
                               accum_out=small[:, s, 4:5]).then_inc(s_exp, 1)
                    activation(SM[:, s, P:P + T], SM[:, s, P:P + T], ACT.Exp, bias=small[:, s, 3:4], scale=SCALE,
                               accum_out=small[:, s, 5:6]).then_inc(s_exp, 1)

                def turned(h):
                    act.wait_ge(t_psum, 4 * i + h + 1)
                    activation(PT[:, h % 2, :], (M3, M1)[h % 2][:, 0:P + T], ACT.Copy).then_inc(pt_ready, 1)

                for j in range(8):
                    split(B_GRP + j, 768 if j < 5 else 1024, 8, i)
                    if j == 0:
                        load_ada(32, 2, i)
                    if j == 1:
                        for f in range(2):
                            evac(B_GRP, f, pair(KN, f), ACT.Copy, 8, i)
                    if j == 2:
                        used(B_GRP + 1, 8, i)
                        activation(V[:, 0, :], M0[:], ACT.Copy).then_inc(mv_ready, 1)
                        activation(V[:, 1, :], M1[:], ACT.Copy).then_inc(mv_ready, 1)
                    if j == 6:
                        evac(B_GRP + 5, 0, pair(QN, 0), ACT.Copy, 8, i)
                exps(0)
                exps(1)
                evac(B_GRP + 7, 1, pair(QN, 1), ACT.Copy, 8, i)
                turned(0)
                turned(1)
                exps(2)
                exps(3)
                turned(2)
                turned(3)
                act.wait_ge(mo_gated, 4 * i + 5)
                activation(dyn(Yh, 4 * i, 4), YG, ACT.Copy).then_inc(yh_ready, 1)
            out_evac(B_MO, S_POST1, 40)
            split(B_PJ1)
            root_of(S_POST1, D)
            split(B_PJ1 + 1)
            for c in range(2):
                for f in (2 * c, 2 * c + 1):
                    evac(B_PJ1 + c, f, pair(PP, f), ACT.Copy)
            pairs_hi(X, x_ready, X_POST1, 2)
            ple_gate(B_PG1, X_PLE1, False)

            def ln(s, n):
                square_pairs(s, Z, n // 2, (centred, sum(LN_PAIRS[:LN_INDEX[s]])))
                root_of(s, n * P, "ln_eps")

            ln(S_LNA, 8)
            pairs_hi(Z, aff, AFF[0], 2)
            with act.Fori(0, 2) as i:
                def value_gate(f, i):
                    act.wait_ge(dve_free, V_WA + 2 + 2 * i)
                    used(B_WA + 2 * f + 1, 4, i)
                    activation(SGT[:, f, 0:T], GD[f][:, T:2 * T], ACT.Sigmoid).then_inc(sgt_ready, 1)

                for j in range(4):
                    split(B_WA + j, 1024, 4, i)
                    if j == 2:
                        value_gate(0, i)
                value_gate(1, i)
            act.wait_ge(pads, 1)
            for j in range(4):
                split(B_WP + j)
                if j == 2:
                    evac(B_WP + 1, 0, U[:, 0:2, 16:16 + T], ACT.Copy)
            evac(B_WP + 3, 1, U[:, 2:4, 16:16 + T], ACT.Copy)
            with act.Fori(0, 4) as i:
                for j in range(4):
                    split(B_WG + j, 1024, 4, i)
                    if j == 2:
                        evac(B_WG + 1, 0, dyn(G, 4 * i, 2), ACT.Sigmoid, 4, i)
                evac(B_WG + 3, 1, dyn(G, 4 * i + 2, 2), ACT.Sigmoid, 4, i)
            act.wait_ge(pooled, 4)
            activation(Sh[:], PO, ACT.Copy).then_inc(pooled_hi, 1)
            split(B_POOL)
            ln(S_CONV, 4)
            for p in range(2):
                act.wait_ge(aff, AFF[1] + 2 * p + 2)
                activation(pair(Z, p), pair(Z, p), ACT.Silu).then_inc(act_conv, 1)
            for p in range(2):
                act.wait_ge(act_conv, p + 1)
                activation(pair(Yh, p), pair(Z, p), ACT.Copy).then_inc(convh_ready, 1)
            for j in range(5):
                if j < 4:
                    split(B_PW + j)
                if j > 0:
                    act.wait_ge(merged_t, j)
                    activation(pair(Hh, j - 1), pair(Z, j - 1), ACT.Copy).then_inc(hh_ready, 1)
            for j in range(4):
                split(B_WO + j)
            for j in range(4):
                split(B_WO + 4 + j)
            ln(S_LN1, 8)
            ln(S_LNB, 8)
            pairs_hi(Z, aff, AFF[3], 2)
            act.wait_ge(pads, 2)
            split(B_UP)
            split(B_UP + 1)
            with act.Fori(0, 11) as i:
                def conv_start(f):
                    used(B_UP + 2 * f + 1, 4, i)
                    for n in range(2):
                        x = 4 * i + 2 * f + n
                        activation(CV[:, 2 * f + n, :], GA[f][:, T * n:T * n + T], ACT.Identity,
                                   bias=dcol("bdwf", x), scale=dcol("dwf", x + 2 * 44)).then_inc(cv0, 1)
                    activation(UPAD[:, 2 * f:2 * f + 2, 2:2 + T], wide(GA[f]), ACT.Copy).then_inc(act_free, 1)

                def gelu(f):
                    act.wait_ge(cv_step, 8 * i + 4 * f + 4)
                    activation(GG[:, f, :], CV[:, 2 * f + 1, :], ACT.Gelu_apprx_tanh).then_inc(gg_ready, 1)

                def hidden_hi(f):
                    act.wait_ge(f_ready, 2 * i + f + 1)
                    activation(dyn(Yh, 2 * i + f, 1), FF[:, f:f + 1, :], ACT.Copy).then_inc(fh_ready, 1)

                for j in range(4):
                    split(B_UP + 2 + j, 1024, 4, i)
                    if j == 0:
                        conv_start(0)
                    if j == 1:
                        gelu(0)
                    if j == 2:
                        hidden_hi(0)
                        conv_start(1)
                    if j == 3:
                        gelu(1)
                        hidden_hi(1)
            with act.Fori(0, 3) as i:
                for j in range(8):
                    split(B_DN + 2 + j, DN_TILES[(j + 1) % 4] * P, 8, i)
            for j in range(3):
                split(B_DN + 26 + j, DN_TILES[(j + 1) % 4] * P)
            ln(S_LN2, 8)

        @block.vector
        def _(dve):
            tt = nc.vector.tensor_tensor
            stt = nc.vector.scalar_tensor_tensor
            ts = nc.vector.tensor_scalar

            def split(base, n=1024, per=0, i=0):
                b = base + AHEAD
                if b >= B_END:
                    return
                s = b % RING
                dve.wait_ge(hi_done, b + 1 + per * i)
                tt(wlo[:, s, 0:n], raw[:, s, 0:n], f32(whi[:, s, 0:n]), ALU.subtract).then_inc(lo_done, 1)

            def used(base, per=0, i=0):
                dve.wait_ge(pe_done, base + RING + 1 + per * i)

            def dyn(a, t, n):
                return a[:, bass.ds(t, n), :]

            def ada(x, n, a, per, i):
                dve.wait_ge(ada_loaded[n], 16 * (x // 2) + 16 + 16 * (per // 2) * i)
                dve.wait_ge(ada_used, x + 2 + per * i)
                stt(ada_acc[:, a, :], ada_raw[:, n, :], siluc[:, bass.ds(2 * i + n, 1)], ada_acc[:, a, :],
                    ALU.mult, ALU.add).then_inc(ada_used, 1)

            def mod_read(call, g, n):
                dve.wait_ge(mod_psum, call + 1)
                tt(mod[:, 8 * g:8 * (g + n)], M2[:, 0:8 * n], col("bada", 8 * g, 8 * n), ALU.add).then_inc(mod_done, 1)
                nc.vector.memset(ada_acc[:, 0, :], 0.0).then_inc(ada_zero, 1)
                dve.wait_ge(ada_zero, call + 2)

            def rope(b, ta, tb, cos, dst, tmp_n, free_sem, free_n, ready, ready_n, per=(0, 0, 0), i=0, frees=1):
                tt(ta, wide(b), over(TAB[:, cos, :], 2), ALU.mult).then_inc(rope_tmp, 1)
                tt(tb, wide(b), over(TAB[:, cos + 1, :], 2), ALU.mult).then_inc(free_sem, frees)
                dve.wait_ge(rope_tmp, tmp_n + per[0] * i)
                dve.wait_ge(free_sem, free_n + per[1] * i)
                tt(dst[:, 0, :], ta[:, 0, :], tb[:, 1, :], ALU.subtract).then_inc(ready, 1)
                tt(dst[:, 1, :], tb[:, 0, :], ta[:, 1, :], ALU.add).then_inc(ready, 1)
                dve.wait_ge(ready, ready_n + per[2] * i)

            def rstd_of(s):
                if s > 0:
                    dve.wait_ge(t_ready, T_BEFORE[s])
                dve.wait_ge(root_done, s + 1)
                nc.vector.reciprocal(rstd[:], root[:]).then_inc(rstd_ready, 1)
                dve.wait_ge(rstd_ready, s + 1)

            def pre_norm(s, v, gain):
                rstd_of(s)
                for p in range(4):
                    tt(pair(Z, p), pair(X, p), over(rstd[:], 2), ALU.mult).then_inc(t_ready, 1)
                dve.wait_ge(t_ready, T_BEFORE[s] + 4)
                for t in range(8):
                    dve.wait_ge(hh_ready, HH_BEFORE[v] + t + 1)
                    op = stt(Hl[:, t, :], Z[:, t, :], col(gain, t), f32(Hh[:, t, :]), ALU.mult, ALU.subtract)
                    if t % 2 == 1:
                        op.then_inc(h_ready, 1)

            def pair_lo(src, p, v):
                dve.wait_ge(hh_ready, HH_BEFORE[v] + p + 1)
                tt(pair(Hl, p), pair(src, p), f32(pair(Hh, p)), ALU.subtract).then_inc(h_ready, 1)

            def post_norm(s, v, gain, z_done, x0):
                rstd_of(s)
                dve.wait_ge(act_free, z_done)
                for p in range(4):
                    tt(pair(Z, p), pair(Z, p), over(rstd[:], 2), ALU.mult).then_inc(t_ready, 1)
                    dve.wait_ge(t_ready, T_BEFORE[s] + p + 1)
                    for t in (2 * p, 2 * p + 1):
                        stt(X[:, t, :], Z[:, t, :], col(gain, t), X[:, t, :], ALU.mult, ALU.add).then_inc(x_ready, 1)
                    if p > 0:
                        dve.wait_ge(x_ready, x0 + 2 * p)
                        pair_lo(X, p - 1, v)
                dve.wait_ge(x_ready, x0 + 8)
                pair_lo(X, 3, v)

            def out_loop(b0, ada0):
                with dve.Fori(0, 4) as i:
                    for j in range(4):
                        split(b0 + j, 1024, 4, i)
                        if j == 3:
                            ada(ada0, 0, 0, 2, i)
                    ada(ada0 + 1, 1, 0, 2, i)

            def ple_update(bg, ag, x0, g0):
                def update(f, i):
                    dve.wait_ge(act_free, ag + f + 3 + 2 * i)
                    sg = SGT[:, f, :].rearrange("p (a t) -> p a t", a=2)
                    tt(sg, sg, dyn(PP, 4 * i + 2 * f, 2), ALU.mult).then_inc(gate_t, 1)
                    dve.wait_ge(gate_t, g0 + 2 * i + f + 1)
                    x = dyn(X, 4 * i + 2 * f, 2)
                    tt(x, x, sg, ALU.add).then_inc(x_ready, 1)

                with dve.Fori(0, 2) as i:
                    for j in range(4):
                        split(bg + j, 1024, 4, i)
                        if j == 2:
                            update(0, i)
                    update(1, i)

            def p_lo(layer):
                dve.wait_ge(ph_ready, layer + 1)
                tt(Sl[:, 0:2, :], praw[:], f32(Sh[:, 0:2, :]), ALU.subtract).then_inc(p_ready, 1)

            nc.vector.memset(prime[:, 0:1], 0.0).then_inc(pe_done, RING)
            nc.vector.memset(prime[:, 1:2], 0.0).then_inc(lo_done, RING)
            nc.vector.memset(prime[:, 2:3], 0.0).then_inc(act_free, 2)
            nc.vector.memset(prime[:, 3:4], 0.0).then_inc(dve_free, 2)
            nc.vector.memset(prime[:, 4:5], 0.0).then_inc(ada_used, 2)
            nc.vector.memset(prime[:, 5:6], 0.0).then_inc(o_free, 1)
            nc.vector.memset(prime[:, 6:7], 0.0).then_inc(groot, 1)
            nc.vector.memset(prime[:, 7:8], 0.0).then_inc(mo_gated, 1)
            nc.vector.memset(ones[:], 1.0).then_inc(const_ready, 1)
            nc.vector.memset(ada_acc[:], 0.0).then_inc(ada_zero, 1)
            dve.wait_ge(ada_zero, 1)
            dve.wait_ge(in_cols, 16)
            dve.wait_ge(in_pos, 16)
            step = [0]

            def chained(op):
                step[0] += 1
                op.then_inc(trig_step, 1)
                dve.wait_ge(trig_step, step[0])

            chained(nc.vector.tensor_copy(posf, posi))
            for n, inv in ((0, "invf_ret"), (2, "invf_mla")):
                chained(ts(rt[:, n, :], posf, col(inv), None, ALU.mult))
                chained(ts(rt[:, n + 1, :], posf, col(inv), None, ALU.mult))
            for n in (0, 2):
                chained(ts(rk[:, n, :], rt[:, n, :], 1.0 / TWO_PI, 0.25, ALU.mult, ALU.add))
                chained(ts(rk[:, n + 1, :], rt[:, n + 1, :], 1.0 / TWO_PI, None, ALU.mult))
            chained(ts(rk, rk, ROUND, None, ALU.add))
            chained(ts(rk, rk, ROUND, None, ALU.subtract))
            for c in TURN:
                chained(stt(rt, rk, -c, rt, ALU.mult, ALU.add))
            for n in (0, 2):
                chained(ts(rt[:, n, :], rt[:, n, :], float(np.float32(np.pi / 2)), None, ALU.add))
            ts(rt, rt, PI_IN, -PI_IN, ALU.min, ALU.max).then_inc(trig_arg, 1)
            for b in range(AHEAD):
                split(b - AHEAD)
            pre_norm(S_PRE0, H_RET, "pre0")
            p_lo(0)
            dve.wait_ge(trig_ready, 1)
            dve.wait_ge(in_const, 16 * 4)
            dve.wait_ge(silu_c, 1)

            with dve.Fori(0, RET_HEADS) as i:
                def gated(t, b):
                    return stt(YF[:, t, :], b[:, T * (t % 2):T * (t % 2) + T], dcol("gn", 4 * i + t), SG[:, t, :],
                               ALU.mult, ALU.mult)

                for j in range(12):
                    split(B_HEAD + j, 1024, 12, i)
                    if j == 2:
                        used(B_HEAD + 1, 12, i)
                        rope(GD[0], TA, TB, 0, Q, 1, dve_free, V_HEAD + 3, rope_ready, 2, (2, 2, 4), i)
                    if j == 4:
                        used(B_HEAD + 3, 12, i)
                        rope(GD[1], TA, TB, 0, K, 2, dve_free, V_HEAD + 4, rope_ready, 4, (2, 2, 4), i)
                    if j == 3:
                        ada(0, 0, 0, 4, i)
                    if j == 5:
                        ada(1, 1, 0, 4, i)
                    if j == 8:
                        dve.wait_ge(at_ready, i + 1)
                        m = maskd[:, bass.ds(i, 1), :].rearrange("p a t -> p (a t)")
                        tt(AT[:, 0:T], M2[:, 0:T], m, ALU.mult).then_inc(atm_ready, 1)
                        tt(AT[:, T:T + P], M2[:, T:T + P], m[:, 0:P], ALU.mult).then_inc(atm_ready, 1)
                        ada(2, 0, 1, 4, i)
                    if j == 9:
                        ada(3, 1, 1, 4, i)
                    if j == 10:
                        dve.wait_ge(act_free, A_HEAD + 3 + 2 * i)
                        dve.wait_ge(gsq, 2 * i + 1)
                        gated(0, M3)
                        gated(1, M3)
                dve.wait_ge(act_free, A_HEAD + 4 + 2 * i)
                dve.wait_ge(gsq, 2 * i + 2)
                gated(2, M2)
                gated(3, M2).then_inc(o_free, 1)
                dve.wait_ge(groot, i + 2)
                nc.vector.reciprocal(rstd[:], root[:]).then_inc(grs, 1)
                dve.wait_ge(grs, i + 1)
                dve.wait_ge(o_free, i + 2)
                tt(YF, YF, over(rstd[:], 4), ALU.mult).then_inc(yf_ready, 1)
                dve.wait_ge(yh_ready, i + 1)
                tt(dyn(Yl, 4 * i, 4), YF, f32(dyn(Yh, 4 * i, 4)), ALU.subtract).then_inc(y_ready, 1)
            mod_read(0, 0, 2)
            out_loop(B_RO, 16)
            mod_read(1, 2, 1)
            split(B_PJ0)
            split(B_PJ0 + 1)
            post_norm(S_POST0, H_PLE0, "post0", A_PJ0 + 2, X_POST0)
            dve.wait_ge(act_free, A_PG0 + 2)
            ple_update(B_PG0, A_PG0, X_PLE0, 0)

            dve.wait_ge(x_ready, X_POST1)
            pre_norm(S_PRE1, H_MLA, "pre1")
            with dve.Fori(0, 2) as i:
                for j in range(4):
                    split(B_MIN + j, 1024, 4, i)
            split(B_MIN + 8)
            split(B_MIN + 9)
            p_lo(1)
            for s, p0, p1 in ((S_Q, 0, 3), (S_KV, 3, 4)):
                rstd_of(s)
                for p in range(p0, p1):
                    tt(pair(Z, p), pair(Z, p), over(rstd[:], 2), ALU.mult).then_inc(t_ready, 1)
            dve.wait_ge(t_ready, T_BEFORE[S_KV] + 1)
            for t in range(8):
                dve.wait_ge(cqh_ready, t + 1)
                h, l, t0, g = (Yh, Yl, 16 + t, col("qn", t)) if t < 6 else (Sh, Sl, t - 4, col("kvn", t - 6))
                stt(l[:, t0, :], Z[:, t, :], g, f32(h[:, t0, :]), ALU.mult, ALU.subtract).then_inc(cq_ready, 1)
            used(B_MIN + 9)
            rope(GD[0], TC[:, 0, :].rearrange("p (a t) -> p a t", a=2), TC[:, 1, :].rearrange("p (a t) -> p a t", a=2),
                 2, KR, 2 * RET_HEADS + 1, dve_free, V_KR + 4, qr_ready, 2, frees=2)
            with dve.Fori(0, 4) as i:
                for j in range(4):
                    split(B_MG + j, 1024, 4, i)
                    if j == 3:
                        ada(24, 0, 0, 2, i)
                ada(25, 1, 0, 2, i)
            mod_read(2, 3, 1)
            with dve.Fori(0, 4) as i:
                def masked(h):
                    dve.wait_ge(s_psum, 4 * i + h + 1)
                    s = h % 2
                    tt(SM[:, s, :], GD[s][:, 0:P + T], tri[:], ALU.add).then_inc(s_masked, 1)
                    dve.wait_ge(s_masked, 4 * i + h + 1)
                    nc.vector.reduce_max(small[:, s, 0:1], SM[:, s, 0:P], AX_X).then_inc(s_max, 1)
                    nc.vector.reduce_max(small[:, s, 1:2], SM[:, s, P:P + T], AX_X).then_inc(s_max, 1)
                    dve.wait_ge(s_max, 8 * i + 2 * h + 2)
                    ts(small[:, s, 2:4], small[:, s, 0:2], -SCALE, None, ALU.mult).then_inc(s_bias, 1)

                def normed(h):
                    dve.wait_ge(s_exp, 8 * i + 2 * h + 2)
                    s = h % 2
                    nc.vector.reciprocal(small[:, s, 6:8], small[:, s, 4:6]).then_inc(s_inv, 1)
                    dve.wait_ge(s_inv, 4 * i + h + 1)
                    ts(SM[:, s, 0:P], SM[:, s, 0:P], small[:, s, 6:7], None, ALU.mult).then_inc(s_prob, 1)
                    ts(SM[:, s, P:P + T], SM[:, s, P:P + T], small[:, s, 7:8], None, ALU.mult).then_inc(s_prob, 1)

                def gate_head(h):
                    dve.wait_ge(mo_psum, 4 * i + h + 1)
                    tt(YG[:, h:h + 1, :], (M2, M0)[h % 2][:, 0:T].unsqueeze(1), dyn(G, 4 * i + h, 1), ALU.mult)\
                        .then_inc(mo_gated, 1)

                for j in range(8):
                    split(B_GRP + j, 768 if j < 5 else 1024, 8, i)
                    if j == 3:
                        ada(32, 0, 0, 2, i)
                    if j == 4:
                        used(B_GRP + 3, 8, i)
                        rope(M2, TC[:, 0, :].rearrange("p (a t) -> p a t", a=2),
                             TC[:, 1, :].rearrange("p (a t) -> p a t", a=2), 2, QR, 2 * RET_HEADS + 2, rope_read, 1,
                             qr_ready, 4, (1, 1, 2), i)
                    if j == 5:
                        ada(33, 1, 0, 2, i)
                masked(0)
                masked(1)
                normed(0)
                normed(1)
                masked(2)
                gate_head(0)
                masked(3)
                gate_head(1)
                normed(2)
                normed(3)
                gate_head(2)
                gate_head(3)
                dve.wait_ge(mo_gated, 4 * i + 5)
                dve.wait_ge(yh_ready, RET_HEADS + i + 1)
                tt(dyn(Yl, 4 * i, 4), YG, f32(dyn(Yh, 4 * i, 4)), ALU.subtract).then_inc(y_ready, 1)
            mod_read(3, 4, 1)
            out_loop(B_MO, 40)
            mod_read(4, 5, 1)
            dve.wait_ge(mod_done, 5)
            for g in (1, 4):
                ts(mod[:, 8 * g:8 * g + 8], mod[:, 8 * g:8 * g + 8], 1.0, None, ALU.add).then_inc(mod_one, 1)
            split(B_PJ1)
            split(B_PJ1 + 1)
            post_norm(S_POST1, H_PLE1, "post1", A_PJ1 + 2, X_POST1)
            dve.wait_ge(act_free, A_PG1 + 2)
            ple_update(B_PG1, A_PG1, X_PLE1, 4)

            def layer_norm(s, src, n, dst, gain, offset, between=None):
                k = LN_INDEX[s]
                c0 = sum(LN_PAIRS[:k])
                dve.wait_ge(mean_psum, k + 1)
                ts(mean[:], M3[:, 0:T], 1.0 / (n * P), None, ALU.mult).then_inc(mean_ready, 1)
                dve.wait_ge(mean_ready, k + 1)
                for p in range(n // 2):
                    tt(pair(Z, p), pair(src, p), over(mean[:], 2), ALU.subtract).then_inc(centred, 1)
                dve.wait_ge(centred, c0 + n // 2)
                if between is not None:
                    between()
                rstd_of(s)
                for p in range(n // 2):
                    tt(pair(Z, p), pair(Z, p), over(rstd[:], 2), ALU.mult).then_inc(t_ready, 1)
                for t in range(n):
                    dve.wait_ge(t_ready, T_BEFORE[s] + t // 2 + 1)
                    ts(dst[:, t, :], Z[:, t, :], gain(t), offset(t), ALU.mult, ALU.add).then_inc(aff, 1)

            dve.wait_ge(x_ready, X_DONE)
            dve.wait_ge(mod_one, 2)
            layer_norm(S_LNA, X, 8, Z, lambda t: mod[:, 8 + t:9 + t], lambda t: mod[:, t:t + 1])
            nc.vector.memset(CI[:, :, 0:30], 0.0).then_inc(ci_pad, 1)
            for p in range(4):
                dve.wait_ge(aff, AFF[0] + 2 * p + 2)
                pair_lo(Z, p, H_CONV)
            dve.wait_ge(ci_pad, 1)
            with dve.Fori(0, 2) as i:
                def gated_value(f, i):
                    dve.wait_ge(sgt_ready, 2 * i + f + 1)
                    tt(CI[:, bass.ds(2 * i + f, 1), 30:30 + T], GD[f][:, 0:T].unsqueeze(1), SGT[:, f:f + 1, 0:T],
                       ALU.mult).then_inc(dve_free, 1)

                for j in range(4):
                    split(B_WA + j, 1024, 4, i)
                    if j == 2:
                        gated_value(0, i)
                gated_value(1, i)
            dve.wait_ge(dve_free, V_WA + 4 + 2)
            ts(X[:], X[:], ALPHA, None, ALU.mult).then_inc(xs_ready, 1)
            for j in range(4):
                split(B_WP + j)
            with dve.Fori(0, 4) as i:
                co = dyn(CO, i, 1)

                def tap(k):
                    x = CI[:, bass.ds(i, 1), k:k + T]
                    if k == 0:
                        ts(co, x, dcol("dwa", CONV_K * i), dcol("bdwa", i), ALU.mult, ALU.add).then_inc(conv_step, 1)
                    else:
                        dve.wait_ge(conv_step, CONV_K * i + k)
                        stt(co, x, dcol("dwa", CONV_K * i + k), co, ALU.mult, ALU.add).then_inc(conv_step, 1)

                for j in range(4):
                    split(B_WG + j, 1024, 4, i)
                    for k in range(8 * j, min(8 * j + 8, CONV_K)):
                        tap(k)
            dve.wait_ge(pooled_hi, 1)
            tt(Sl[:], PO, f32(Sh[:]), ALU.subtract).then_inc(pooled_ready, 1)
            split(B_POOL)
            dve.wait_ge(conv_step, CONV_K * CONV_TILES)
            def pool_branch():
                used(B_POOL)
                dve.wait_ge(act_free, A_UP + 2)
                for n in range(8):
                    op = stt(G[:, 8 + n, :], bank[2 + n // 2][:, T * (n % 2):T * (n % 2) + T], col("ps", n),
                             G[:, 8 + n, :], ALU.mult, ALU.mult)
                    if n % 2 == 1:
                        op.then_inc(dve_free, 1)

            layer_norm(S_CONV, CO, 4, Z, lambda t: col("lnag", t), lambda t: col("lnab", t), pool_branch)
            for p in range(2):
                dve.wait_ge(convh_ready, p + 1)
                tt(pair(Yl, p), pair(Z, p), f32(pair(Yh, p)), ALU.subtract).then_inc(conv_ready, 1)
            for j in range(6):
                if j < 4:
                    split(B_PW + j)
                if 1 <= j < 5:
                    p = j - 1
                    used(B_PW + p)
                    tt(pair(Z, p), wide(GD[(V_PW + p) % 2]), pair(G, p), ALU.mult).then_inc(dve_free, 1)
                    dve.wait_ge(dve_free, V_PW + p + 3)
                    tt(pair(Z, p), pair(Z, p), pair(G, 4 + p), ALU.add).then_inc(merged_t, 1)
                if j > 1:
                    dve.wait_ge(merged_t, j - 1)
                    pair_lo(Z, j - 2, H_MERGED)

            def residual(b, o, t, gate_col):
                x = dyn(X, t, 1)
                return stt(x, o.unsqueeze(1), mod[:, bass.ds(t + gate_col, 1)], x, ALU.mult, ALU.add)

            dve.wait_ge(xs_ready, 1)
            with dve.Fori(0, 2) as i:
                def mixed(f, i):
                    used(B_WO + 2 * f + 1, 4, i)
                    residual(None, GD[f][:, 0:T], 4 * i + 2 * f, 16)
                    residual(None, GD[f][:, T:2 * T], 4 * i + 2 * f + 1, 16).then_inc(dve_free, 1)

                for j in range(4):
                    split(B_WO + j, 1024, 4, i)
                    if j == 2:
                        mixed(0, i)
                mixed(1, i)
            dve.wait_ge(dve_free, V_DN + 2)
            layer_norm(S_LN1, X, 8, X, lambda t: col("ln1g", t), lambda t: col("ln1b", t))
            dve.wait_ge(aff, AFF[3])
            layer_norm(S_LNB, X, 8, Z, lambda t: mod[:, 32 + t:33 + t], lambda t: mod[:, 24 + t:25 + t])
            for p in range(4):
                dve.wait_ge(aff, AFF[3] + 2 * p + 2)
                pair_lo(Z, p, H_FF)
            ts(X[:], X[:], ALPHA, None, ALU.mult).then_inc(xs_ready, 1)
            nc.vector.memset(UPAD[:, :, 0:2], 0.0).then_inc(pads, 1)
            split(B_UP)
            split(B_UP + 1)
            with dve.Fori(0, 11) as i:
                def older_taps(f):
                    for k in (1, 0):
                        for n in range(2):
                            c = 2 * f + n
                            if k == 1:
                                dve.wait_ge(cv0, 4 * i + c + 1)
                                if n == 0:
                                    dve.wait_ge(act_free, A_UP + f + 3 + 2 * i)
                            else:
                                dve.wait_ge(cv_step, 8 * i + 4 * f + n + 1)
                            stt(CV[:, c, :], UPAD[:, c, k:k + T], dcol("dwf", 4 * i + c + 44 * k), CV[:, c, :],
                                ALU.mult, ALU.add).then_inc(cv_step, 1)

                def hidden(f):
                    dve.wait_ge(gg_ready, 2 * i + f + 1)
                    tt(FF[:, f, :], GG[:, f, :], CV[:, 2 * f, :], ALU.mult).then_inc(f_ready, 1)

                def hidden_lo(f):
                    dve.wait_ge(fh_ready, 2 * i + f + 1)
                    tt(dyn(Yl, 2 * i + f, 1), FF[:, f:f + 1, :], f32(dyn(Yh, 2 * i + f, 1)), ALU.subtract)\
                        .then_inc(fl_ready, 1)

                for j in range(4):
                    split(B_UP + 2 + j, 1024, 4, i)
                    if j == 0:
                        older_taps(0)
                    if j == 1:
                        hidden(0)
                    if j == 2:
                        hidden_lo(0)
                        older_taps(1)
                    if j == 3:
                        hidden(1)
                        hidden_lo(1)

            def down(t, i, per):
                used(B_DN + 4 * t + 3, per, i)
                residual(None, GD[t][:, 0:T], 2 * i + t if per else 6 + t, 40).then_inc(dve_free, 1)

            dve.wait_ge(xs_ready, 2)
            with dve.Fori(0, 3) as i:
                for j in range(8):
                    split(B_DN + 2 + j, DN_TILES[(j + 1) % 4] * P, 8, i)
                    if j == 2:
                        down(0, i, 8)
                    if j == 6:
                        down(1, i, 8)
            for j in range(3):
                split(B_DN + 26 + j, DN_TILES[(j + 1) % 4] * P)
            for t in range(2):
                used(B_DN + 24 + 4 * t + 3)
                stt(X[:, 6 + t, :], GD[t][:, 0:T], mod[:, 46 + t:47 + t], X[:, 6 + t, :], ALU.mult, ALU.add)\
                    .then_inc(dve_free, 1)
            dve.wait_ge(dve_free, V_DN + 8 + 2)
            layer_norm(S_LN2, X, 8, X, lambda t: col("ln2g", t), lambda t: col("ln2b", t))

        @block.gpsimd
        def _(pool):
            step = [0]

            def chained(op):
                step[0] += 1
                op.then_inc(pool_step, 1)
                pool.wait_ge(pool_step, step[0])

            pool.wait_ge(dve_free, V_WA + 3)
            nc.gpsimd.memset(U[:, :, 0:16], 0.0).then_inc(pads, 1)
            pool.wait_ge(pads, 1)
            pool.wait_ge(act_free, A_WP + 2 + 2)
            for g, window in enumerate(WINDOWS):
                src, shift, n = U[:, g, :], 1, 0
                while shift < window:
                    lo = 2 * shift - 1
                    dst = W1[:, n % 2, :]
                    chained(nc.gpsimd.tensor_tensor(dst[:, lo:16 + T], src[:, lo:16 + T], src[:, lo - shift:16 + T - shift],
                                                    ALU.add))
                    src, shift, n = dst, 2 * shift, n + 1
                chained(nc.gpsimd.tensor_tensor(src[:, 16:32], src[:, 16:32], cnt[:, g, :], ALU.mult))
                chained(nc.gpsimd.tensor_scalar(src[:, 16:16 + T], src[:, 16:16 + T], 1.0 / window, None, ALU.mult))
                nc.gpsimd.tensor_tensor(PO[:, g, :], src[:, 16:16 + T], U[:, g, 16:16 + T], ALU.subtract).then_inc(pooled, 1)
                pool.wait_ge(pooled, g + 1)


def _features(a):
    return np.ascontiguousarray(a.T.reshape(-1, P, a.shape[0]).transpose(1, 0, 2))


def _tiles(a):
    return a.reshape(a.shape[0] // P, P, a.shape[1] // P, P)


def _strips(a, kts=None):
    t = _tiles(a)
    return t.transpose(2, 1, 0, 3).reshape(t.shape[2], P, -1)


def _deep(a):
    t = _strips(a)
    return t.reshape(t.shape[0], P, 2, 1024).transpose(0, 2, 1, 3).reshape(-1, P, 1024)


def _short(a, per):
    t = _strips(a)
    return t.reshape(-1, per, P, t.shape[2]).transpose(0, 2, 1, 3).reshape(-1, P, per * t.shape[2])


def _rows(a):
    return a.reshape(-1, 2, P, 512).transpose(0, 2, 1, 3).reshape(-1, P, 1024)


def _col(a):
    return a.reshape(-1, P).T


def kernel(x, p, positions, pre_norm_g, post_norm_g, ret_w_in, ret_gn_g, ret_w_out, mla_w_in, mla_q_norm_g,
           mla_kv_norm_g, mla_w_uq, mla_w_uk, mla_w_uv, mla_w_out, ple_w_proj, ple_w_gate, c_2, w_ada_2, b_ada_2,
           w_in_2, w_dw_a_2, b_dw_a_2, ln_a_g_2, ln_a_b_2, w_pw_a_2, w_pool_2, pool_scale_2, w_out_2, ln1_g_2, ln1_b_2,
           w_up_2, w_dw_f_2, b_dw_f_2, w_down_2, ln2_g_2, ln2_b_2):
    import concourse.bacc as bacc
    from concourse.bass_utils import run_bass_kernel_spmd

    f = np.float32
    cat = np.concatenate

    wi = ret_w_in[0]
    heads = []
    for h in range(RET_HEADS):
        heads += [_strips(wi[:, 256 * h:256 * h + 256]), _strips(wi[:, 1024 + 256 * h:1280 + 256 * h]),
                  _rows(wi[:, 2048 + 512 * h:2560 + 512 * h]), _strips(wi[:, 4096 + 512 * h:4608 + 512 * h])]
    mi = mla_w_in[0]
    kr = mi[:, 1024:1088]
    kr = cat([kr[:, 0:32]] * 4 + [kr[:, 32:64]] * 4, axis=1)
    uq = mla_w_uq[0].reshape(768, MLA_HEADS, MLA_NOPE + MLA_ROPE)
    uk = mla_w_uk[0].reshape(256, MLA_HEADS * MLA_NOPE)
    uv = mla_w_uv[0].reshape(256, MLA_HEADS * 128)
    uqs = []
    for g in range(4):
        hs = uq[:, 4 * g:4 * g + 4]
        uqs += [_strips(hs[:, :, 128:160].reshape(768, 128)), _strips(hs[:, :, 160:192].reshape(768, 128)),
                _strips(hs[:, :, 0:128].reshape(768, 512))]
    w2 = w_in_2[0]
    av, ag = _strips(w2[:, 0:512]), _strips(w2[:, 512:1024])
    up = _strips(w_up_2[0])
    order = [x for t in range(FF_TILES) for x in (t, FF_TILES + t)]
    down = _strips(w_down_2[0])
    downs, k0 = [], 0
    for n in DN_TILES:
        part = down[:, :, k0 * P:(k0 + n) * P]
        downs.append(cat([part, np.zeros((DT, P, (6 - n) * P), f)], axis=2) if n < 6 else part)
        k0 += n
    weights = {
        "head": cat(heads), "ret_out": _deep(ret_w_out[0]), "proj0": _short(ple_w_proj[0], 4),
        "ple_gate0": _strips(ple_w_gate[0]), "mla_qkv": _strips(mi[:, 0:1024]), "mla_kr": _strips(kr),
        "mla_gate": _strips(mi[:, 1088:]), "uk": _short(uk, 4),
        "uv": cat([_rows(uv[:, 512 * g:512 * g + 512]) for g in range(4)]), "uq": cat(uqs),
        "mla_out": _deep(mla_w_out[0]), "proj1": _short(ple_w_proj[1], 4), "ple_gate1": _strips(ple_w_gate[1]),
        "conv_in": np.stack([av, ag], axis=1).reshape(8, P, 1024), "pool_in": _strips(w2[:, 1024:1536]),
        "gates": _strips(w2[:, 1536:]),
        "pool_w": w_pool_2[0].reshape(4, P, 2, P).transpose(1, 0, 2, 3).reshape(1, P, 1024),
        "pw": _short(w_pw_a_2[0], 2), "mix": _strips(w_out_2[0]), "up": up[order],
        "down": np.stack(downs, axis=1).reshape(-1, P, 768),
    }
    ada = w_ada_2[0].reshape(8, P, 6, 1024).transpose(2, 0, 1, 3)
    ada = cat([ada[0:2].reshape(2, 4, 2, P, 1024).transpose(1, 0, 2, 3, 4).reshape(16, P, 1024),
               ada[2:].reshape(32, P, 1024)])

    half_r, half_m = 128, 32
    inv_r = (10000.0 ** (-np.arange(half_r, dtype=np.float64) / half_r)).astype(f)
    inv_m = np.tile((10000.0 ** (-np.arange(half_m, dtype=np.float64) / half_m)).astype(f), 4)
    rel = np.arange(T)[None, :] - np.arange(P)[:, None]
    decay = [1.0 - 2.0 ** (-5.0 - h) for h in range(RET_HEADS)]
    mask = np.stack([np.where(rel >= 0, g ** np.maximum(rel, 0), 0.0) / 16.0 for g in decay], axis=1).astype(f)
    diagonal = np.where(np.arange(P)[None, :] <= np.arange(P)[:, None], 0.0, NEG).astype(f)
    tri = cat([diagonal, np.zeros((P, P), f), diagonal], axis=1)
    cnt = np.stack([n / np.minimum(np.arange(16) + 1, n) for n in WINDOWS]).astype(f)
    cnt = np.ascontiguousarray(np.broadcast_to(cnt, (P, 4, 16)))

    dwf = cat([_col(w_dw_f_2[0][k])[:, order] for k in range(3)], axis=1)
    dwa = w_dw_a_2[0].reshape(CONV_K, CONV_TILES, P).transpose(2, 1, 0).reshape(P, -1)
    cols = cat([_col(pre_norm_g[0]), _col(pre_norm_g[1]), _col(post_norm_g[0]), _col(post_norm_g[1]), _col(ret_gn_g[0]),
                _col(mla_q_norm_g[0]), _col(mla_kv_norm_g[0]), _col(b_ada_2[0]), _col(c_2[0]), dwa, _col(b_dw_a_2[0]),
                _col(ln_a_g_2[0]), _col(ln_a_b_2[0]), _col(pool_scale_2[0]), _col(ln1_g_2[0]), _col(ln1_b_2[0]), dwf,
                _col(b_dw_f_2[0])[:, order], _col(ln2_g_2[0]), _col(ln2_b_2[0]), inv_r[:, None], inv_m[:, None],
                np.full((P, 1), RMS_EPS, f), np.full((P, 1), LN_EPS, f)], axis=1)

    arrays = {
        "x_in": _features(x[0]), "p_in": np.stack([_features(p[0, 0]), _features(p[1, 0])]), "pos_in": positions[0],
        "cols_in": cols, "mask_in": mask, "tri_in": tri, "cnt_in": cnt, "ident_in": np.eye(P, dtype=f), "ada_in": ada,
    }
    arrays.update({"w_" + n: a for n, a in weights.items()})
    arrays = {n: np.ascontiguousarray(a) for n, a in arrays.items()}
    nc = bacc.Bacc("TRN2", target_bir_lowering=False, num_devices=1)
    ap = {n: nc.dram_tensor(n, a.shape, mybir.dt.from_np(a.dtype), kind="ExternalInput").ap() for n, a in arrays.items()}
    out = nc.dram_tensor("out", (P, DT, T), F32, kind="ExternalOutput").ap()
    program(nc, ap["x_in"], ap["p_in"], ap["pos_in"], ap["cols_in"], ap["mask_in"], ap["tri_in"], ap["cnt_in"],
            ap["ident_in"], ap["ada_in"], {n: ap["w_" + n] for n in weights}, out)
    got = run_bass_kernel_spmd(nc, [arrays], core_ids=[0]).results[0]["out"]
    return np.ascontiguousarray(got.transpose(1, 0, 2).reshape(D, T).T)[None]
```

```python
from contextlib import ExitStack

import numpy as np

import concourse.bass as bass
from concourse import mybir

F32 = mybir.dt.float32
F32R = mybir.dt.float32r
I32 = mybir.dt.int32
ALU = mybir.AluOpType
AX_X = mybir.AxisListType.X
ACT = mybir.ActivationFunctionType

P = 128
T = 256
D = 1024
DT = D // P
RING = 4
AHEAD = 3
RET_HEADS, RET_V = 4, 512
MLA_HEADS, MLA_NOPE, MLA_ROPE = 16, 128, 64
Q_TILES, KV_TILES = 6, 2
CONV_K, CONV_TILES = 31, 4
WINDOWS = (2, 4, 8, 16)
FF_TILES = 22
SCALE = (MLA_NOPE + MLA_ROPE) ** -0.5
ALPHA = 2.0 ** 0.25
RMS_EPS, LN_EPS = 1e-6, 1e-5
TWO_PI = 2.0 * np.pi
NEG = -3.0e38

COLS = {}
_n = 0
for _name, _w in (("pre0", 8), ("pre1", 8), ("post0", 8), ("post1", 8), ("gn", 16), ("qn", 6), ("kvn", 2),
                  ("bada", 48), ("c", 8), ("dwa", CONV_TILES * CONV_K), ("bdwa", 4), ("lnag", 4), ("lnab", 4),
                  ("ps", 8), ("ln1g", 8), ("ln1b", 8), ("dwf", 44 * 3), ("bdwf", 44), ("ln2g", 8), ("ln2b", 8),
                  ("invf_ret", 1), ("invf_mla", 1), ("rms_eps", 1), ("ln_eps", 1)):
    COLS[_name] = _n
    _n += _w
NCOLS = _n

B_HEAD = 0
B_RO = B_HEAD + 12 * RET_HEADS
B_PJ0 = B_RO + 16
B_PG0 = B_PJ0 + 2
B_MIN = B_PG0 + 8
B_MG = B_MIN + 10
B_GRP = B_MG + 4
B_MO = B_GRP + 44
B_PJ1 = B_MO + 16
B_PG1 = B_PJ1 + 2
B_WA = B_PG1 + 8
B_WP = B_WA + 8
B_WG = B_WP + 4
B_POOL = B_WG + 16
B_PW = B_POOL + 1
B_WO = B_PW + 4
B_UP = B_WO + 8
B_DN = B_UP + 2 * FF_TILES
B_END = B_DN + 4 * DT
DN_TILES = (6, 6, 5, 5)

A_HEAD = 0
A_RO = A_HEAD + 2 * RET_HEADS
A_PJ0 = A_RO + 8
A_PG0 = A_PJ0 + 4
A_MIN = A_PG0 + 4
A_MG = A_MIN + 4
A_GRP = A_MG + 2
A_MO = A_GRP + 22
A_PJ1 = A_MO + 8
A_PG1 = A_PJ1 + 4
A_WP = A_PG1 + 4
A_WG = A_WP + 2
A_UP = A_WG + 8
V_HEAD = 0
V_KR = V_HEAD + 2 * RET_HEADS
V_WA = V_KR + 2
V_POOL = V_WA + 4
V_PW = V_POOL + 4
V_WO = V_PW + 4
V_DN = V_WO + 4

S_PRE0, S_POST0, S_PRE1, S_Q, S_KV, S_POST1, S_LNA, S_CONV, S_LN1, S_LNB, S_LN2 = range(11)
SQ_INCS = (4, 8, 4, 3, 1, 8, 4, 2, 4, 4, 4)


def sq_before(s):
    return sum(SQ_INCS[:s])


LN_PAIRS = (4, 2, 4, 4, 4)
LN_INDEX = {S_LNA: 0, S_CONV: 1, S_LN1: 2, S_LNB: 3, S_LN2: 4}

H_RET, H_PLE0, H_MLA, H_PLE1, H_CONV, H_MERGED, H_FF = range(7)

X_POST0, X_PLE0, X_POST1, X_PLE1, X_DONE = 0, 8, 12, 20, 24
AFF = (0, 8, 8, 16, 24)
AFF_END = 32
T_BEFORE = (0, 4, 8, 12, 15, 16, 20, 24, 26, 30, 34)
HH_BEFORE = (0, 8, 12, 20, 24, 28, 32)
TURN = (6.28125, float(np.float32(0.0019350051879882812)), 2.0 * np.pi - 6.28125 - 0.0019350051879882812)
ROUND = 1.5 * 2.0 ** 23
PI_IN = 3.1415925


def program(nc, x_in, p_in, pos_in, cols_in, mask_in, tri_in, cnt_in, ident_in, ada_in, w, out):
    ctx = ExitStack()
    with ctx:
        def sb(name, shape, dt=F32):
            return ctx.enter_context(nc.sbuf_tensor(name, shape, dt))

        def sem(name):
            return ctx.enter_context(nc.semaphore(name))

        raw = sb("raw", [P, RING, 1024])
        whi = sb("whi", [P, RING, 1024], F32R)
        wlo = sb("wlo", [P, RING, 1024], F32R)
        ada_raw = sb("ada_raw", [P, 2, 1024])
        ada_acc = sb("ada_acc", [P, 2, 1024])
        X = sb("X", [P, DT, T])
        Hh = sb("Hh", [P, DT, T], F32R)
        Hl = sb("Hl", [P, DT, T], F32R)
        Yh = sb("Yh", [P, FF_TILES, T], F32R)
        Yl = sb("Yl", [P, FF_TILES, T], F32R)
        Sh = sb("Sh", [P, 4, T], F32R)
        Sl = sb("Sl", [P, 4, T], F32R)
        Z = sb("Z", [P, DT, T])
        G = sb("G", [P, 16, T])
        praw = sb("praw", [P, 2, T])
        WK = sb("WK", [P, 20, T])
        TAB = sb("TAB", [P, 4, T])
        maskd = sb("maskd", [P, RET_HEADS, T])
        tri = sb("tri", [P, 3 * P])
        cnt = sb("cnt", [P, 4, 16])
        cols = sb("cols", [P, NCOLS])
        ident = sb("ident", [P, P])
        ones = sb("ones", [P, P])
        mod = sb("mod", [P, 48])
        siluc = sb("siluc", [P, 8])
        root = sb("root", [P, T])
        rstd = sb("rstd", [P, T])
        SGT = sb("SGT", [P, 2, 512])
        small = sb("small", [P, 2, 8])
        prime = sb("prime", [P, 8])
        warm = sb("warm", [P, S_LN2 + 1])
        pool_prime = sb("pool_prime", [P, 1])

        PP = WK[:, 0:8, :]
        SQ = WK[:, 8:16, :]
        Q, K = WK[:, 0:2, :], WK[:, 2:4, :]
        V = WK[:, 4:8, :].rearrange("p a t -> p (a t)").rearrange("p (t v) -> p t v", t=2)
        AT = WK[:, 16:18, :].rearrange("p a t -> p (a t)")
        TA = WK[:, 12:14, :]
        TB = WK[:, 14:16, :]
        SG = G[:, 0:4, :]
        YF = G[:, 4:8, :]
        KR = WK[:, 18:20, :]
        QN, KN = WK[:, 0:4, :], WK[:, 8:12, :]
        QR = WK[:, 12:14, :]
        SM = WK[:, 14:17, :].rearrange("p a t -> p (a t)").rearrange("p (s n) -> p s n", s=2)
        PT = Z[:, 0:3, :].rearrange("p a t -> p (a t)").rearrange("p (s n) -> p s n", s=2)
        YG = Z[:, 4:8, :]
        TC = SGT
        CI = WK[:, 0:5, :].rearrange("p a t -> p (a t)")[:, 0:4 * 286].rearrange("p (c n) -> p c n", c=4)
        CO = WK[:, 16:20, :]
        U = WK[:, 5:10, :].rearrange("p a t -> p (a t)")[:, 0:4 * 272].rearrange("p (c n) -> p c n", c=4)
        W1 = WK[:, 10:13, :].rearrange("p a t -> p (a t)")[:, 0:2 * 272].rearrange("p (c n) -> p c n", c=2)
        TP = WK[:, 13:16, :]
        PO = Z[:, 4:8, :]
        UPAD = WK[:, 0:5, :].rearrange("p a t -> p (a t)")[:, 0:4 * 258].rearrange("p (c n) -> p c n", c=4)
        CV = WK[:, 8:12, :]
        GG = WK[:, 12:14, :]
        FF = WK[:, 14:16, :]
        posi, posf = WK[:, 0, :].bitcast(I32), G[:, 12, :]
        rk, rt = WK[:, 16:18, :], WK[:, 4:6, :]
        mk, mt, mp = G[:, 8:10, :], G[:, 10:12, :], G[:, 14:16, :]

        bank = [ctx.enter_context(nc.psum_tensor(f"bank{i}", [P, 512], F32)) for i in range(8)]
        GA, GD = bank[0:2], bank[2:4]
        M0, M1, M2, M3 = bank[4:8]

        raw_loaded = [sem(f"raw_loaded{s}") for s in range(RING)]
        lo_done, hi_done, pe_done = sem("lo_done"), sem("hi_done"), sem("pe_done")
        act_free, dve_free = sem("act_free"), sem("dve_free")
        ada_loaded = [sem(f"ada_loaded{s}") for s in range(2)]
        ada_used, mod_psum, mod_done = sem("ada_used"), sem("mod_psum"), sem("mod_done")
        ada_zero = sem("ada_zero")
        in_cols, in_pos, in_const, in_p = sem("in_cols"), sem("in_pos"), sem("in_const"), sem("in_p")
        in_x, in_x1 = sem("in_x"), sem("in_x1")
        const_ready = sem("const_ready")
        trig_step, trig_arg, trig_ready = sem("trig_step"), sem("trig_arg"), sem("trig_ready")
        silu_c, mla_arg, mla_step = sem("silu_c"), sem("mla_arg"), sem("mla_step")
        sq_ready, stat_ready, root_done, rstd_ready = sem("sq_ready"), sem("stat_ready"), sem("root_done"), sem("rstd_ready")
        mean_psum, centred = sem("mean_psum"), sem("centred")
        t_ready, hh_ready, h_ready = sem("t_ready"), sem("hh_ready"), sem("h_ready")
        rope_tmp, rope_ready = sem("rope_tmp"), sem("rope_ready")
        v_ready, at_ready, atm_ready = sem("v_ready"), sem("at_ready"), sem("atm_ready")
        o_ready, o_free = sem("o_ready"), sem("o_free")
        gsq, gstat, groot, grs = sem("gsq"), sem("gstat"), sem("groot"), sem("grs")
        yf_ready, yh_ready, y_ready = sem("yf_ready"), sem("yh_ready"), sem("y_ready")
        ph_ready, p_ready, rope_read, mod_one, ci_pad = (sem("ph_ready"), sem("p_ready"), sem("rope_read"), sem("mod_one"),
                                                        sem("ci_pad"))
        x_ready, gate_t = sem("x_ready"), sem("gate_t")
        sgt_ready = sem("sgt_ready")
        cqh_ready, cq_ready = sem("cqh_ready"), sem("cq_ready")
        mv_ready, qr_ready = sem("mv_ready"), sem("qr_ready")
        s_psum, s_masked, s_bias, s_exp, s_inv, s_prob = (sem("s_psum"), sem("s_masked"), sem("s_bias"), sem("s_exp"),
                                                        sem("s_inv"), sem("s_prob"))
        s_max = sem("s_max")
        t_psum, pt_ready, mo_psum, mo_gated = sem("t_psum"), sem("pt_ready"), sem("mo_psum"), sem("mo_gated")
        pool_step, pooled, pooled_hi, pooled_ready = sem("pool_step"), sem("pooled"), sem("pooled_hi"), sem("pooled_ready")
        conv_step, act_conv, convh_ready, conv_ready, aff = (sem("conv_step"), sem("act_conv"), sem("convh_ready"),
                                                             sem("conv_ready"), sem("aff"))
        merged_t, xs_ready, pads = sem("merged_t"), sem("xs_ready"), sem("pads")
        tap_ready, conv_sum = sem("tap_ready"), sem("conv_sum")
        cv0, cv_step, gg_ready = sem("cv0"), sem("cv_step"), sem("gg_ready")
        f_ready, fh_ready, fl_ready = sem("f_ready"), sem("fh_ready"), sem("fl_ready")
        stored = sem("stored")

        def col(name, t=0, n=1):
            return cols[:, COLS[name] + t:COLS[name] + t + n]

        def dcol(name, t):
            return cols[:, bass.ds(t + COLS[name], 1)] if not isinstance(t, int) else col(name, t)

        def pair(a, t):
            return a[:, 2 * t:2 * t + 2, :]

        def wide(b):
            return b[:].rearrange("p (a t) -> p a t", a=2)

        def over(a, n):
            return a.unsqueeze(1).to_broadcast([P, n, T])

        def f32(a):
            return a.bitcast(F32)

        block = ctx.enter_context(nc.Block())

        def finish(sp):
            for t in range(4):
                sp.wait_ge(aff, AFF_END - 8 + 2 * t + 2)
                sp.dma_start(out[:, 2 * t:2 * t + 2, :], pair(X, t)).then_inc(stored, 16)
            sp.wait_ge(stored, 16 * 4)

        @block.sync
        def _(sp):
            def load(base, src, n, per=0, i=0):
                s = base % RING
                sp.wait_ge(lo_done, base + 1 + per * i)
                sp.dma_start(raw[:, s, 0:n], src).then_inc(raw_loaded[s], 16)

            def load_loop(base, name, count, per):
                blocks, n = w[name], w[name].shape[2]
                with sp.Fori(0, count) as i:
                    for j in range(per):
                        load(base + j, blocks[bass.ds(per * i + j, 1)].rearrange("b p n -> p (b n)"), n, per, i)

            def load_all(base, name):
                blocks, n = w[name], w[name].shape[2]
                for j in range(blocks.shape[0]):
                    load(base + j, blocks[j], n)

            sp.dma_start(cols[:], cols_in).then_inc(in_cols, 16)
            sp.dma_start(posi, pos_in.partition_broadcast(P)).then_inc(in_pos, 16)
            sp.dma_start(X[:, 0:4, :], x_in[:, 0:4, :]).then_inc(in_x, 16)
            sp.dma_start(X[:, 4:8, :], x_in[:, 4:8, :]).then_inc(in_x1, 16)
            load_loop(B_HEAD, "head", RET_HEADS, 12)
            load_loop(B_RO, "ret_out", 4, 4)
            load_all(B_PJ0, "proj0")
            load_loop(B_PG0, "ple_gate0", 2, 4)
            sp.wait_ge(p_ready, 1)
            sp.dma_start(praw[:], p_in[1]).then_inc(in_p, 16)
            load_loop(B_MIN, "mla_qkv", 2, 4)
            for j in range(2):
                load(B_MIN + 8 + j, w["mla_kr"][j], 1024)
            for j in range(4):
                load(B_MG + j, w["mla_gate"][j], 1024)

            def load_group(o, i, gates):
                def one(name, k):
                    return w[name][bass.ds(k, 1)].rearrange("b p n -> p (b n)")

                load(B_GRP + 12 * o, one("uk", i + o), 1024, 12, i)
                load(B_GRP + 12 * o + 1, one("uv", i + o), 1024, 12, i)
                for j in range(6):
                    load(B_GRP + 12 * o + 2 + j, one("uq", 6 * i + 6 * o + j), 768, 12, i)
                for j in range(4 if gates else 0):
                    load(B_GRP + 12 * o + 8 + j, one("mla_gate", 4 * i + 4 * o + 4 + j), 1024, 12, i)

            with sp.Fori(0, 3) as i:
                load_group(0, i, True)
            load_group(3, 0, False)
            load_loop(B_MO, "mla_out", 4, 4)
            load_all(B_PJ1, "proj1")
            load_loop(B_PG1, "ple_gate1", 2, 4)
            load_loop(B_WA, "conv_in", 2, 4)
            load_all(B_WP, "pool_in")
            load_loop(B_WG, "gates", 4, 4)
            load_all(B_POOL, "pool_w")
            load_all(B_PW, "pw")
            load_loop(B_WO, "mix", 2, 4)
            load_loop(B_UP, "up", 11, 4)
            with sp.Fori(0, 4) as i:
                for j in range(8):
                    n = DN_TILES[j % 4] * P
                    load(B_DN + j, w["down"][bass.ds(8 * i + j, 1)].rearrange("b p n -> p (b n)")[:, 0:n], n, 8, i)
            finish(sp)

        @block.tensor
        def _(pe):
            mm = nc.tensor.matmul

            def products(base, parts, per=0, i=0, before=()):
                s = base % RING
                pe.wait_ge(lo_done, base + RING + 1 + per * i)
                for n, (t, ah, al, o, start, stop) in enumerate(parts):
                    if n < len(before) and before[n]:
                        pe.wait_ge(*before[n])
                    c = slice(t * P, t * P + P)
                    mm(o, whi[:, s, c], ah, start=start, stop=False)
                    mm(o, whi[:, s, c], al, start=False, stop=False)
                    last = mm(o, wlo[:, s, c], ah, start=False, stop=stop)
                last.then_inc(pe_done, 1)

            def strip(base, o, ah, al, per=0, i=0, before=()):
                products(base, [(k, ah[:, k, :], al[:, k, :], o, k == 0, k == 7) for k in range(8)], per, i, before)

            def free_a(k, per=0, i=0):
                pe.wait_ge(act_free, k + 1 + per * i)
                return GA[k % 2]

            def free_d(k, per=0, i=0):
                pe.wait_ge(dve_free, k + 1 + per * i)
                return GD[k % 2]

            def halves(b):
                return b[:, 0:T], b[:, T:2 * T]

            def h_waits(v):
                return [(h_ready, 4 * v + k // 2 + 1) if k % 2 == 0 else None for k in range(8)]

            def stats(s, n, b=None, tiles=None):
                b = M3 if b is None else b
                if s > 0:
                    pe.wait_ge(root_done, s)
                for k in range(n) if tiles is None else tiles:
                    if k * SQ_INCS[s] % n == 0:
                        pe.wait_ge(sq_ready, sq_before(s) + k * SQ_INCS[s] // n + 1)
                    last = mm(b[:, 0:T], ones[:], SQ[:, k, :], start=(k == (tiles or [0])[0]),
                              stop=(k == (tiles[-1] if tiles else n - 1)))
                last.then_inc(stat_ready, 1)

            def mean_sum(src, tiles, ready):
                pe.wait_ge(mod_done, 4)
                for k in tiles:
                    pe.wait_ge(*ready(k))
                    last = mm(M2[:, 0:T], ones[:], src[:, k, :], start=(k == tiles[0]), stop=(k == tiles[-1]))
                last.then_inc(mean_psum, 1)

            def mod_columns(g, n, call):
                pe.wait_ge(ada_used, 2 + 8 * (g + n))
                if call > 0:
                    pe.wait_ge(mod_done, call)
                for a in range(n):
                    for t in range(8):
                        last = mm(M2[:, 8 * a + t:8 * a + t + 1], ada_acc[:, a, t * P:t * P + P], ones[:, 0:1],
                                  start=True, stop=True)
                last.then_inc(mod_psum, 1)

            def out_product(b0, a0, y0):
                with pe.Fori(0, 4) as i:
                    for t in range(2):
                        o = free_a(a0 + t, 2, i)[:, 0:T]
                        for c in range(2):
                            parts = [(k, Yh[:, 8 * c + k, :], Yl[:, 8 * c + k, :], o, c == 0 and k == 0, c == 1 and k == 7)
                                     for k in range(8)]
                            products(b0 + 2 * t + c, parts, 4, i, [(y_ready, y0 + 2 * c + 2)])

            def per_layer(s, bp, ap, bg, ag, v, layer, g, call):
                for c in range(2):
                    parts = []
                    for n in range(4):
                        o = GA[(ap + 2 * c + n // 2) % 2][:, T * (n % 2):T * (n % 2) + T]
                        parts += [(2 * n + k, Sh[:, k, :], Sl[:, k, :], o, k == 0, k == 1) for k in range(2)]
                    if c == 0:
                        pe.wait_ge(p_ready, layer + 1)
                    pe.wait_ge(act_free, ap + 2 * c + 1)
                    products(bp + c, parts, before=[None] * 4 + [(act_free, ap + 2 * c + 2)])
                    if c == 0:
                        stats(s, 8)
                mod_columns(g, 1, call)
                with pe.Fori(0, 2) as i:
                    for j in range(4):
                        if j % 2 == 0:
                            b = free_a(ag + j // 2, 2, i)
                        strip(bg + j, halves(b)[j % 2], Hh, Hl, 4, i, h_waits(v) if j == 0 else ())

            def strips_a(base, a, count, v=None):
                with pe.Fori(0, count) as i:
                    for j in range(4):
                        if j % 2 == 0:
                            b = free_a(a + j // 2, 2, i)
                        strip(base + j, halves(b)[j % 2], Hh, Hl, 4, i, h_waits(v) if v is not None and j == 0 else ())

            def strips_d(base, d, count, v):
                with pe.Fori(0, count) as i:
                    for j in range(4):
                        if j % 2 == 0:
                            b = free_d(d + j // 2, 2, i)
                        strip(base + j, halves(b)[j % 2], Hh, Hl, 4, i, h_waits(v) if j == 0 else ())

            pe.wait_ge(const_ready, 1)
            stats(S_PRE0, 8)

            with pe.Fori(0, RET_HEADS) as i:
                for j in range(4):
                    if j % 2 == 0:
                        b = free_d(V_HEAD + j // 2, 2, i)
                    strip(B_HEAD + j, halves(b)[j % 2], Hh, Hl, 12, i, h_waits(H_RET) if j == 0 else ())
                pe.wait_ge(groot, i + 1)
                for j in range(4):
                    base = B_HEAD + 4 + j
                    s = base % RING
                    pe.wait_ge(lo_done, base + RING + 1 + 12 * i)
                    for k in range(2):
                        kk = 2 * j + k
                        c = slice(512 * k, 512 * k + 512)
                        for t, o in ((0, M0), (1, M1)):
                            tt = slice(P * t, P * t + P)
                            mm(o[:], Hh[:, kk, tt], whi[:, s, c], start=(kk == 0), stop=False)
                            mm(o[:], Hh[:, kk, tt], wlo[:, s, c], start=False, stop=False)
                            last = mm(o[:], Hl[:, kk, tt], whi[:, s, c], start=False, stop=(kk == 7))
                    last.then_inc(pe_done, 1)
                pe.wait_ge(rope_ready, 4 * i + 4)
                pe.wait_ge(o_free, i + 1)
                for d in range(2):
                    mm(M2[:, 0:T], K[:, d, 0:P], Q[:, d, :], start=(d == 0), stop=(d == 1))
                for d in range(2):
                    last = mm(M2[:, T:T + P], K[:, d, P:T], Q[:, d, P:T], start=(d == 0), stop=(d == 1))
                last.then_inc(at_ready, 1)
                b = free_a(A_HEAD, 2, i)
                strip(B_HEAD + 8, halves(b)[0], Hh, Hl, 12, i)
                strip(B_HEAD + 9, halves(b)[1], Hh, Hl, 12, i)
                pe.wait_ge(v_ready, 2 * i + 2)
                pe.wait_ge(atm_ready, 2 * i + 2)
                for t in range(4):
                    o = (M3, M2)[t // 2][:, T * (t % 2):T * (t % 2) + T]
                    c = slice(P * t, P * t + P)
                    mm(o, V[:, 0, c], AT[:, 0:T], start=True, stop=False)
                    last = mm(o[:, P:T], V[:, 1, c], AT[:, T:T + P], start=False, stop=True)
                    if t % 2 == 1:
                        last.then_inc(o_ready, 1)
                b = free_a(A_HEAD + 1, 2, i)
                strip(B_HEAD + 10, halves(b)[0], Hh, Hl, 12, i)
                pe.wait_ge(gsq, 2 * i + 2)
                for t in range(4):
                    last = mm(M1[:, 0:T], ones[:], SQ[:, t, :], start=(t == 0), stop=(t == 3))
                last.then_inc(gstat, 1)
                strip(B_HEAD + 11, halves(b)[1], Hh, Hl, 12, i)
            pe.wait_ge(o_free, RET_HEADS + 1)
            mod_columns(0, 2, 0)
            out_product(B_RO, A_RO, 0)
            per_layer(S_POST0, B_PJ0, A_PJ0, B_PG0, A_PG0, H_PLE0, 0, 2, 1)

            stats(S_PRE1, 8)
            strips_a(B_MIN, A_MIN, 2, H_MLA)
            b = free_d(V_KR)
            strip(B_MIN + 8, halves(b)[0], Hh, Hl)
            stats(S_Q, 6, tiles=list(range(6)))
            pe.wait_ge(sq_ready, sq_before(S_KV + 1))
            pe.wait_ge(mod_done, 2)
            for k in (6, 7):
                last = mm(M2[:, 0:T], ones[:], SQ[:, k, :], start=(k == 6), stop=(k == 7))
            last.then_inc(stat_ready, 1)
            strip(B_MIN + 9, halves(b)[1], Hh, Hl)
            for j in range(4):
                if j % 2 == 0:
                    b = free_a(A_MG + j // 2)
                strip(B_MG + j, halves(b)[j % 2], Hh, Hl)
            pe.wait_ge(root_done, S_KV + 1)
            pe.wait_ge(cq_ready, Q_TILES + KV_TILES)
            pe.wait_ge(dve_free, V_WA + 2)

            def group(o, i, gates):
                base = B_GRP + 12 * o

                def at(n, per):
                    return n + per * o + per * i

                parts = []
                for h in range(4):
                    out_k = GA[h // 2][:, T * (h % 2):T * (h % 2) + T]
                    parts += [(2 * h + k, Sh[:, 2 + k, :], Sl[:, 2 + k, :], out_k, k == 0, k == 1) for k in range(2)]
                pe.wait_ge(act_free, at(A_GRP + 1, 6))
                products(base, parts, 12, i, [None] * 4 + [(act_free, at(A_GRP + 2, 6))])
                pe.wait_ge(mo_gated, at(1, 4))
                s = (base + 1) % RING
                pe.wait_ge(lo_done, base + 1 + RING + 1 + 12 * i)
                for k in range(2):
                    c = slice(512 * k, 512 * k + 512)
                    for t, v in ((0, M0), (1, M1)):
                        tt = slice(P * t, P * t + P)
                        mm(v[:], Sh[:, 2 + k, tt], whi[:, s, c], start=(k == 0), stop=False)
                        mm(v[:], Sh[:, 2 + k, tt], wlo[:, s, c], start=False, stop=False)
                        last = mm(v[:], Sl[:, 2 + k, tt], whi[:, s, c], start=False, stop=(k == 1))
                last.then_inc(pe_done, 1)

                def latent_strip(j, b):
                    products(base + j, [(k, Yh[:, 16 + k, :], Yl[:, 16 + k, :], b, k == 0, k == 5) for k in range(6)],
                             12, i)

                def gate_strip(j):
                    if gates:
                        if j % 2 == 0:
                            pe.wait_ge(act_free, at(A_GRP + 5 + j // 2, 6))
                        strip(base + 8 + j, halves(GA[j // 2])[j % 2], Hh, Hl, 12, i)

                def scores(h):
                    if h >= 2:
                        pe.wait_ge(s_masked, at(h - 1, 4))
                    r = slice(32 * h, 32 * h + 32)
                    for q0, n, b in ((0, P, GD[h % 2][:, 0:P]), (P, T, GD[h % 2][:, P:P + T])):
                        mm(b, QN[:, h, q0:q0 + P], KN[:, h, 0:n], start=True, stop=False)
                        mm(b, QR[r, 0, q0:q0 + P], KR[r, 0, 0:n], start=False, stop=False)
                        last = mm(b, QR[r, 1, q0:q0 + P], KR[r, 1, 0:n], start=False, stop=True)
                    last.then_inc(s_psum, 1)

                def turn(h):
                    pe.wait_ge(s_prob, at(2 * h + 2, 8))
                    if h >= 2:
                        pe.wait_ge(pt_ready, at(h - 1, 4))
                    b = (M3, M1)[h % 2]
                    nc.tensor.transpose(b[:, 0:P], SM[:, h % 2, 0:P], ident[:])
                    nc.tensor.transpose(b[:, P:T], SM[:, h % 2, P:T], ident[:])
                    nc.tensor.transpose(b[:, T:T + P], SM[:, h % 2, T:T + P], ident[:]).then_inc(t_psum, 1)

                def values(h):
                    pe.wait_ge(pt_ready, at(h + 1, 4))
                    if h >= 2:
                        pe.wait_ge(mo_gated, at(h, 4))
                    b = (M2, M0)[h % 2][:, 0:T]
                    c = slice(P * h, P * h + P)
                    mm(b, V[:, 0, c], PT[:, h % 2, 0:T], start=True, stop=False)
                    mm(b[:, P:T], V[:, 1, c], PT[:, h % 2, T:T + P], start=False, stop=True).then_inc(mo_psum, 1)

                latent_strip(2, M2[:, 0:T])
                latent_strip(3, M2[:, T:2 * T])
                pe.wait_ge(act_free, at(A_GRP + 3, 6))
                latent_strip(4, GA[0][:, 0:T])
                latent_strip(5, GA[0][:, T:2 * T])
                pe.wait_ge(act_free, at(A_GRP + 4, 6))
                latent_strip(6, GA[1][:, 0:T])
                pe.wait_ge(qr_ready, at(4, 2))
                pe.wait_ge(act_free, at(A_GRP + 5, 6))
                scores(0)
                scores(1)
                latent_strip(7, GA[1][:, T:2 * T])
                gate_strip(0)
                pe.wait_ge(act_free, at(A_GRP + 6, 6))
                scores(2)
                scores(3)
                pe.wait_ge(mv_ready, at(2, 2))
                turn(0)
                turn(1)
                gate_strip(1)
                values(0)
                values(1)
                gate_strip(2)
                turn(2)
                turn(3)
                gate_strip(3)
                values(2)
                values(3)

            with pe.Fori(0, 3) as i:
                group(0, i, True)
            group(3, 0, False)
            pe.wait_ge(mo_gated, 4 * 4 + 1)
            mod_columns(3, 2, 2)
            out_product(B_MO, A_MO, 4)
            per_layer(S_POST1, B_PJ1, A_PJ1, B_PG1, A_PG1, H_PLE1, 1, 5, 3)

            mean_sum(X, range(8), lambda k: (x_ready, X_PLE1 + k // 2 + 1))
            stats(S_LNA, 8)
            strips_d(B_WA, V_WA, 2, H_CONV)
            strips_a(B_WP, A_WP, 1)
            strips_a(B_WG, A_WG, 4)
            mean_sum(CO, (3, 0, 1, 2), lambda k: (conv_step, 3 * CONV_K - 2 + k) if k < 3 else (conv_sum, CONV_K))
            stats(S_CONV, 4)
            pe.wait_ge(pooled_ready, 1)
            pe.wait_ge(dve_free, V_POOL + 2)
            products(B_POOL, [(n, Sh[:, n // 2, :], Sl[:, n // 2, :], halves(bank[2 + n // 2])[n % 2], True, True)
                              for n in range(8)])
            for j in range(4):
                b = free_d(V_PW + j)
                products(B_PW + j, [(4 * n + k, Yh[:, k, :], Yl[:, k, :], halves(b)[n], k == 0, k == 3)
                                    for n in range(2) for k in range(4)],
                         before=((conv_ready, 1), None, (conv_ready, 2)) if j == 0 else ())
            strips_d(B_WO, V_WO, 2, H_MERGED)
            mean_sum(X, range(8), lambda k: (dve_free, V_WO + 2 + k // 2 + 1))
            stats(S_LN1, 8)
            mean_sum(X, range(8), lambda k: (aff, AFF[2] + k + 1))
            stats(S_LNB, 8)
            strips_a(B_UP, A_UP, 11, H_FF)
            with pe.Fori(0, 4) as i:
                for t in range(2):
                    o = free_d(V_DN + t, 2, i)[:, 0:T]
                    k0 = 0
                    for c, n in enumerate(DN_TILES):
                        parts = [(k, Yh[:, k0 + k, :], Yl[:, k0 + k, :], o, k0 + k == 0, k0 + k == FF_TILES - 1)
                                 for k in range(n)]
                        products(B_DN + 4 * t + c, parts, 8, i, [(fl_ready, (k0 + n + 1) // 2)])
                        k0 += n
            mean_sum(X, range(8), lambda k: (dve_free, V_DN + 2 + k + 1))
            stats(S_LN2, 8)

        @block.scalar
        def _(act):
            activation = nc.scalar.activation

            def split(base, n=1024, per=0, i=0):
                b = base + AHEAD
                if b >= B_END:
                    return
                s = b % RING
                act.wait_ge(raw_loaded[s], 16 * (b // RING) + 16 + 16 * (per // RING) * i)
                act.wait_ge(pe_done, b + 1 + per * i)
                activation(whi[:, s, 0:n], raw[:, s, 0:n], ACT.Copy).then_inc(hi_done, 1)

            def used(base, per=0, i=0):
                act.wait_ge(pe_done, base + RING + 1 + per * i)

            def load_ada(x, per, i):
                for n in range(2):
                    act.wait_ge(ada_used, x + n + 1 + per * i)
                    act.dma_start(ada_raw[:, n, :], ada_in[bass.ds(per * i + x + n, 1)].rearrange("b p n -> p (b n)"))\
                       .then_inc(ada_loaded[n], 16)

            def square_pairs(s, src, n, ready=None):
                if s > 0:
                    act.wait_ge(stat_ready, s)
                for p in range(n):
                    if ready is not None:
                        act.wait_ge(ready[0], ready[1] + p + 1)
                    activation(pair(SQ, p), pair(src, p), ACT.Square).then_inc(sq_ready, 1)

            def sqrt_table(s):
                if s == 0:
                    act.wait_ge(const_ready, 1)
                activation(warm[:, s:s + 1], ones[:, 0:1], ACT.Sqrt)

            def root_of(s, n, eps="rms_eps", b=None):
                if s > 0:
                    act.wait_ge(rstd_ready, s)
                act.wait_ge(stat_ready, s + 1)
                activation(root[:], (M3 if b is None else b)[:, 0:T], ACT.Sqrt, bias=col(eps), scale=1.0 / n)\
                    .then_inc(root_done, 1)

            def scaled_hi(src, dst, gain, t0, n, out_sem, base):
                for t in range(n):
                    if t % 2 == 0:
                        act.wait_ge(t_ready, base + t // 2 + 1)
                    activation(dst[:, t0 + t, :], src[:, t, :], ACT.Copy, scale=col(gain, t)).then_inc(out_sem, 1)

            def pairs_hi(src, ready, base, step):
                for p in range(4):
                    act.wait_ge(ready, base + step * (p + 1))
                    activation(pair(Hh, p), pair(src, p), ACT.Copy).then_inc(hh_ready, 1)

            def dyn(a, t, n):
                return a[:, bass.ds(t, n), :]

            def out_evac(b0, s, ada0):
                act.wait_ge(stat_ready, s)

                def tile_out(t, i):
                    used(b0 + 2 * t + 1, 4, i)
                    o = GA[t][:, 0:T].unsqueeze(1)
                    activation(dyn(SQ, 2 * i + t, 1), o, ACT.Square).then_inc(sq_ready, 1)
                    activation(dyn(Z, 2 * i + t, 1), o, ACT.Copy).then_inc(act_free, 1)

                with act.Fori(0, 4) as i:
                    for j in range(4):
                        split(b0 + j, 1024, 4, i)
                        if j == 0:
                            load_ada(ada0, 2, i)
                        if j == 2:
                            tile_out(0, i)
                    tile_out(1, i)

            def ple_gate(bg, x0, squares):
                def gate(f, i):
                    act.wait_ge(x_ready, x0 + 2 * i)
                    used(bg + 2 * f + 1, 4, i)
                    activation(SGT[:, f, :], GA[f][:], ACT.Sigmoid).then_inc(act_free, 1)

                def square(f, i):
                    act.wait_ge(x_ready, x0 + 2 * i + f + 1)
                    activation(dyn(SQ, 4 * i + 2 * f, 2), dyn(X, 4 * i + 2 * f, 2), ACT.Square).then_inc(sq_ready, 1)

                with act.Fori(0, 2) as i:
                    for j in range(4):
                        split(bg + j, 1024, 4, i)
                        if j == 2:
                            gate(0, i)
                        if j == 3 and squares:
                            square(0, i)
                    gate(1, i)
                    if squares:
                        square(1, i)

            def p_hi(layer):
                act.wait_ge(in_p, 16 * layer + 16)
                activation(Sh[:, 0:2, :], praw[:], ACT.Copy).then_inc(ph_ready, 1)

            def evac(base, f, dst, func, per=0, i=0):
                used(base, per, i)
                activation(dst, wide(GA[f % 2]), func).then_inc(act_free, 1)

            for p in range(4):
                act.wait_ge((in_x, in_x1)[p // 2], 16)
                activation(pair(SQ, p), pair(X, p), ACT.Square).then_inc(sq_ready, 1)
            act.dma_start(maskd[:], mask_in).then_inc(in_const, 16)
            act.dma_start(tri[:], tri_in).then_inc(in_const, 16)
            act.dma_start(cnt[:], cnt_in).then_inc(in_const, 16)
            act.dma_start(ident[:], ident_in).then_inc(in_const, 16)
            act.dma_start(praw[:], p_in[0]).then_inc(in_p, 16)
            act.wait_ge(in_cols, 16)
            sqrt_table(S_PRE0)
            split(-3)
            root_of(S_PRE0, D)
            split(-2)
            act.wait_ge(trig_arg, 1)
            activation(TAB[:, 0:2, :], rt, ACT.Sin).then_inc(trig_ready, 1)
            scaled_hi(Z, Hh, "pre0", 0, DT, hh_ready, T_BEFORE[S_PRE0])
            split(-1)
            p_hi(0)
            activation(siluc[:], col("c", 0, 8), ACT.Silu).then_inc(silu_c, 1)

            with act.Fori(0, RET_HEADS) as i:
                for j in range(12):
                    split(B_HEAD + j, 1024, 12, i)
                    if j in (0, 5):
                        load_ada(0 if j == 0 else 2, 4, i)
                    if j == 8:
                        used(B_HEAD + 7, 12, i)
                        activation(V[:, 0, :], M0[:], ACT.Copy).then_inc(v_ready, 1)
                        activation(V[:, 1, :], M1[:], ACT.Copy).then_inc(v_ready, 1)
                    if j == 10:
                        evac(B_HEAD + 9, 0, SG[:, 0:2, :], ACT.Silu, 12, i)
                        for f, b in ((0, M3), (1, M2)):
                            act.wait_ge(o_ready, 2 * i + f + 1)
                            activation(pair(SQ, f), wide(b), ACT.Square).then_inc(gsq, 1)
                    if j == 11:
                        act.wait_ge(gstat, i + 1)
                        activation(root[:], M1[:, 0:T], ACT.Sqrt, bias=col("rms_eps"), scale=1.0 / RET_V).then_inc(groot, 1)
                evac(B_HEAD + 11, 1, SG[:, 2:4, :], ACT.Silu, 12, i)
                act.wait_ge(yf_ready, i + 1)
                activation(dyn(Yh, 4 * i, 4), YF, ACT.Copy).then_inc(yh_ready, 1)
            act.wait_ge(mla_arg, 1)
            activation(TAB[:, 2:4, :], mt, ACT.Sin).then_inc(trig_ready, 1)
            out_evac(B_RO, S_POST0, 16)
            split(B_PJ0)
            sqrt_table(S_POST0)
            root_of(S_POST0, D)
            split(B_PJ0 + 1)
            for c in range(2):
                for f in (2 * c, 2 * c + 1):
                    evac(B_PJ0 + c, f, pair(PP, f), ACT.Copy)
            pairs_hi(X, x_ready, X_POST0, 2)
            ple_gate(B_PG0, X_PLE0, True)

            sqrt_table(S_PRE1)
            root_of(S_PRE1, D)
            scaled_hi(Z, Hh, "pre1", 0, DT, hh_ready, T_BEFORE[S_PRE1])
            with act.Fori(0, 2) as i:
                for j in range(4):
                    split(B_MIN + j, 1024, 4, i)
                    if j == 2:
                        used(B_MIN + 1, 4, i)
                        activation(dyn(SQ, 4 * i, 2), wide(GA[0]), ACT.Square).then_inc(sq_ready, 1)
                        activation(dyn(Z, 4 * i, 2), wide(GA[0]), ACT.Copy).then_inc(act_free, 1)
                used(B_MIN + 3, 4, i)
                activation(dyn(SQ, 4 * i + 2, 2), wide(GA[1]), ACT.Square).then_inc(sq_ready, 1)
                activation(dyn(Z, 4 * i + 2, 2), wide(GA[1]), ACT.Copy).then_inc(act_free, 1)
            split(B_MIN + 8)
            split(B_MIN + 9)
            p_hi(1)
            sqrt_table(S_Q)
            root_of(S_Q, Q_TILES * P)
            root_of(S_KV, KV_TILES * P, b=M2)
            scaled_hi(Z, Yh, "qn", 16, Q_TILES, cqh_ready, T_BEFORE[S_Q])
            scaled_hi(Z[:, 6:8, :], Sh, "kvn", 2, KV_TILES, cqh_ready, T_BEFORE[S_KV])
            act.wait_ge(trig_ready, 2)
            for j in range(4):
                split(B_MG + j)
                if j == 2:
                    evac(B_MG + 1, 0, pair(G, 0), ACT.Silu)
            evac(B_MG + 3, 1, pair(G, 1), ACT.Silu)

            def group(o, i, gates):
                base = B_GRP + 12 * o

                def at(n, per):
                    return n + per * o + per * i

                def exps(h):
                    act.wait_ge(s_bias, at(h + 1, 4))
                    s = h % 2
                    activation(SM[:, s, 0:P], SM[:, s, 0:P], ACT.Exp, bias=small[:, s, 2:3], scale=SCALE,
                               accum_out=small[:, s, 4:5]).then_inc(s_exp, 1)
                    activation(SM[:, s, P:P + T], SM[:, s, P:P + T], ACT.Exp, bias=small[:, s, 3:4], scale=SCALE,
                               accum_out=small[:, s, 5:6]).then_inc(s_exp, 1)

                def turned(h):
                    act.wait_ge(t_psum, at(h + 1, 4))
                    activation(PT[:, h % 2, :], (M3, M1)[h % 2][:, 0:P + T], ACT.Copy).then_inc(pt_ready, 1)

                for j in range(12 if gates else 8):
                    split(base + j, 768 if j < 5 else 1024, 12, i)
                    if j in (0, 5):
                        load_ada((24 if j == 0 else 26) + 4 * o, 4, i)
                    if j == 1:
                        for f in range(2):
                            evac(base, f, pair(KN, f), ACT.Copy, 12, i)
                    if j == 2:
                        used(base + 1, 12, i)
                        activation(V[:, 0, :], M0[:], ACT.Copy).then_inc(mv_ready, 1)
                        activation(V[:, 1, :], M1[:], ACT.Copy).then_inc(mv_ready, 1)
                    if j == 6:
                        evac(base + 5, 0, pair(QN, 0), ACT.Copy, 12, i)
                    if j == 8:
                        evac(base + 7, 1, pair(QN, 1), ACT.Copy, 12, i)
                        exps(0)
                        exps(1)
                    if j == 9:
                        turned(0)
                        turned(1)
                    if j == 10:
                        exps(2)
                        exps(3)
                    if j == 11:
                        evac(base + 9, 0, dyn(G, 4 * i + 4 * o + 4, 2), ACT.Silu, 12, i)
                        turned(2)
                        turned(3)
                if gates:
                    evac(base + 11, 1, dyn(G, 4 * i + 4 * o + 6, 2), ACT.Silu, 12, i)
                else:
                    evac(base + 7, 1, pair(QN, 1), ACT.Copy, 12, i)
                    for h in range(4):
                        exps(h)
                        if h % 2 == 1:
                            turned(h - 1)
                            turned(h)
                act.wait_ge(mo_gated, at(5, 4))
                activation(dyn(Yh, 4 * i + 4 * o, 4), YG, ACT.Copy).then_inc(yh_ready, 1)

            with act.Fori(0, 3) as i:
                group(0, i, True)
            group(3, 0, False)
            out_evac(B_MO, S_POST1, 40)
            split(B_PJ1)
            sqrt_table(S_POST1)
            root_of(S_POST1, D)
            split(B_PJ1 + 1)
            for c in range(2):
                for f in (2 * c, 2 * c + 1):
                    evac(B_PJ1 + c, f, pair(PP, f), ACT.Copy)
            pairs_hi(X, x_ready, X_POST1, 2)
            ple_gate(B_PG1, X_PLE1, False)

            def ln(s, n, dst=None, gain=None, offset=None, v=None):
                square_pairs(s, Z, n // 2, (centred, sum(LN_PAIRS[:LN_INDEX[s]])))
                sqrt_table(s)
                root_of(s, n * P, "ln_eps")
                if dst is None:
                    return
                a0 = AFF[LN_INDEX[s]]
                for t in range(n):
                    if t % 2 == 0:
                        act.wait_ge(t_ready, T_BEFORE[s] + t // 2 + 1)
                    activation(dst[:, t, :], Z[:, t, :], ACT.Identity, bias=offset(t), scale=gain(t)).then_inc(aff, 1)
                    if v is not None and t % 2 == 1:
                        act.wait_ge(aff, a0 + t + 1)
                        activation(pair(Hh, t // 2), pair(dst, t // 2), ACT.Copy).then_inc(hh_ready, 1)

            act.wait_ge(mod_one, 2)
            ln(S_LNA, 8, Z, lambda t: mod[:, 8 + t:9 + t], lambda t: mod[:, t:t + 1], H_CONV)
            with act.Fori(0, 2) as i:
                def value_gate(f, i):
                    act.wait_ge(dve_free, V_WA + 2 + 2 * i)
                    used(B_WA + 2 * f + 1, 4, i)
                    activation(SGT[:, f, 0:T], GD[f][:, T:2 * T], ACT.Sigmoid).then_inc(sgt_ready, 1)

                for j in range(4):
                    split(B_WA + j, 1024, 4, i)
                    if j == 2:
                        value_gate(0, i)
                value_gate(1, i)
            act.wait_ge(pads, 1)

            def tap(k, i=0, per=0):
                x = CI[:, 3, bass.ds(k + per * i, T)]
                w_tap = dcol("dwa", CONV_K * 3 + k + per * i)
                if per == 0 and k == 0:
                    activation(CO[:, 3, :], x, ACT.Identity, bias=col("bdwa", 3), scale=w_tap).then_inc(tap_ready, 1)
                else:
                    if per or k > 3:
                        act.wait_ge(conv_sum, k - 2 + per * i)
                    activation(TP[:, k % 3, :], x, ACT.Copy, scale=w_tap).then_inc(tap_ready, 1)

            act.wait_ge(dve_free, V_WA + 4 + 2)
            for j in range(4):
                split(B_WP + j)
                if j == 2:
                    evac(B_WP + 1, 0, U[:, 0:2, 16:16 + T], ACT.Copy)
                tap(j)
            evac(B_WP + 3, 1, U[:, 2:4, 16:16 + T], ACT.Copy)
            for k in range(4, 7):
                tap(k)
            with act.Fori(0, 4) as i:
                for j in range(4):
                    split(B_WG + j, 1024, 4, i)
                    for k in ((7,), (8, 9), (10,), (11, 12))[j]:
                        tap(k, i, 6)
                    if j == 2:
                        evac(B_WG + 1, 0, dyn(G, 4 * i, 2), ACT.Sigmoid, 4, i)
                evac(B_WG + 3, 1, dyn(G, 4 * i + 2, 2), ACT.Sigmoid, 4, i)
            act.wait_ge(pooled, 4)
            activation(Sh[:], PO, ACT.Copy).then_inc(pooled_hi, 1)
            split(B_POOL)
            ln(S_CONV, 4)
            for t in range(4):
                if t % 2 == 0:
                    act.wait_ge(t_ready, T_BEFORE[S_CONV] + t // 2 + 1)
                activation(Z[:, t, :], Z[:, t, :], ACT.Silu, bias=col("lnab", t), scale=col("lnag", t)).then_inc(act_conv, 1)
                if t % 2 == 1:
                    act.wait_ge(act_conv, t + 1)
                    activation(pair(Yh, t // 2), pair(Z, t // 2), ACT.Copy).then_inc(convh_ready, 1)
            for j in range(5):
                if j < 4:
                    split(B_PW + j)
                if j > 0:
                    act.wait_ge(merged_t, j)
                    activation(pair(Hh, j - 1), pair(Z, j - 1), ACT.Copy).then_inc(hh_ready, 1)
            for j in range(4):
                split(B_WO + j)
            for j in range(4):
                split(B_WO + 4 + j)
            ln(S_LN1, 8, X, lambda t: col("ln1g", t), lambda t: col("ln1b", t))
            ln(S_LNB, 8, Z, lambda t: mod[:, 32 + t:33 + t], lambda t: mod[:, 24 + t:25 + t], H_FF)
            act.wait_ge(pads, 2)
            split(B_UP)
            split(B_UP + 1)
            def gelu(n):
                act.wait_ge(cv_step, 8 * n)
                activation(GG, CV.rearrange("p (f n) t -> p f n t", n=2)[:, :, 1, :], ACT.Gelu_apprx_tanh).then_inc(gg_ready, 1)

            def hidden_hi(n, k):
                act.wait_ge(f_ready, n)
                activation(dyn(Yh, k, 2), FF, ACT.Copy).then_inc(fh_ready, 1)

            def up_pass(o, i):
                def conv_start(f):
                    used(B_UP + 4 * o + 2 * f + 1, 4, i)
                    for n in range(2):
                        x = 4 * i + 4 * o + 2 * f + n
                        activation(CV[:, 2 * f + n, :], GA[f][:, T * n:T * n + T], ACT.Identity,
                                   bias=dcol("bdwf", x), scale=dcol("dwf", x + 2 * 44)).then_inc(cv0, 1)
                    activation(UPAD[:, 2 * f:2 * f + 2, 2:2 + T], wide(GA[f]), ACT.Copy).then_inc(act_free, 1)

                if o:
                    gelu(i + o)
                split(B_UP + 4 * o + 2, 1024, 4, i)
                if o:
                    act.wait_ge(f_ready, i + o)
                conv_start(0)
                split(B_UP + 4 * o + 3, 1024, 4, i)
                if o:
                    hidden_hi(i + o, 2 * i + 2 * o - 2)
                split(B_UP + 4 * o + 4, 1024, 4, i)
                conv_start(1)
                split(B_UP + 4 * o + 5, 1024, 4, i)

            up_pass(0, 0)
            with act.Fori(0, 10) as i:
                up_pass(1, i)
            gelu(11)
            hidden_hi(11, FF_TILES - 2)
            with act.Fori(0, 3) as i:
                for j in range(8):
                    split(B_DN + 2 + j, DN_TILES[(j + 1) % 4] * P, 8, i)
            for j in range(3):
                split(B_DN + 26 + j, DN_TILES[(j + 1) % 4] * P)
            ln(S_LN2, 8, X, lambda t: col("ln2g", t), lambda t: col("ln2b", t))

        @block.vector
        def _(dve):
            tt = nc.vector.tensor_tensor
            stt = nc.vector.scalar_tensor_tensor
            ts = nc.vector.tensor_scalar

            def split(base, n=1024, per=0, i=0):
                b = base + AHEAD
                if b >= B_END:
                    return
                s = b % RING
                dve.wait_ge(hi_done, b + 1 + per * i)
                tt(wlo[:, s, 0:n], raw[:, s, 0:n], f32(whi[:, s, 0:n]), ALU.subtract).then_inc(lo_done, 1)

            def used(base, per=0, i=0):
                dve.wait_ge(pe_done, base + RING + 1 + per * i)

            def dyn(a, t, n):
                return a[:, bass.ds(t, n), :]

            def ada(x, n, a, per, i, o=0):
                dve.wait_ge(ada_loaded[n], 16 * (x // 2) + 16 + 16 * (per // 2) * i)
                dve.wait_ge(ada_used, x + 2 + per * i)
                stt(ada_acc[:, a, :], ada_raw[:, n, :], siluc[:, bass.ds(2 * i + 2 * o + n, 1)], ada_acc[:, a, :],
                    ALU.mult, ALU.add).then_inc(ada_used, 1)

            def mod_read(call, g, n):
                dve.wait_ge(mod_psum, call + 1)
                tt(mod[:, 8 * g:8 * (g + n)], M2[:, 0:8 * n], col("bada", 8 * g, 8 * n), ALU.add).then_inc(mod_done, 1)
                nc.vector.memset(ada_acc[:], 0.0).then_inc(ada_zero, 1)
                dve.wait_ge(ada_zero, call + 2)

            def rope(b, ta, tb, cos, dst, tmp_n, free_sem, free_n, ready, ready_n, per=(0, 0, 0), i=0, frees=1):
                tt(ta, wide(b), over(TAB[:, cos, :], 2), ALU.mult).then_inc(rope_tmp, 1)
                tt(tb, wide(b), over(TAB[:, cos + 1, :], 2), ALU.mult).then_inc(free_sem, frees)
                dve.wait_ge(rope_tmp, tmp_n + per[0] * i)
                dve.wait_ge(free_sem, free_n + per[1] * i)
                tt(dst[:, 0, :], ta[:, 0, :], tb[:, 1, :], ALU.subtract).then_inc(ready, 1)
                tt(dst[:, 1, :], tb[:, 0, :], ta[:, 1, :], ALU.add).then_inc(ready, 1)
                dve.wait_ge(ready, ready_n + per[2] * i)

            def rstd_of(s):
                if s > 0:
                    dve.wait_ge(t_ready, T_BEFORE[s])
                dve.wait_ge(root_done, s + 1)
                nc.vector.reciprocal(rstd[:], root[:]).then_inc(rstd_ready, 1)
                dve.wait_ge(rstd_ready, s + 1)

            def pre_norm(s, v, gain):
                rstd_of(s)
                for p in range(5):
                    if p < 4:
                        tt(pair(Z, p), pair(X, p), over(rstd[:], 2), ALU.mult).then_inc(t_ready, 1)
                    for t in (2 * p - 2, 2 * p - 1) if p else ():
                        dve.wait_ge(t_ready, T_BEFORE[s] + p)
                        dve.wait_ge(hh_ready, HH_BEFORE[v] + t + 1)
                        op = stt(Hl[:, t, :], Z[:, t, :], col(gain, t), f32(Hh[:, t, :]), ALU.mult, ALU.subtract)
                    if p:
                        op.then_inc(h_ready, 1)

            def pair_lo(src, p, v):
                dve.wait_ge(hh_ready, HH_BEFORE[v] + p + 1)
                tt(pair(Hl, p), pair(src, p), f32(pair(Hh, p)), ALU.subtract).then_inc(h_ready, 1)

            def post_norm(s, v, gain, z_done, x0):
                rstd_of(s)
                dve.wait_ge(act_free, z_done)
                for p in range(4):
                    tt(pair(Z, p), pair(Z, p), over(rstd[:], 2), ALU.mult).then_inc(t_ready, 1)
                    dve.wait_ge(t_ready, T_BEFORE[s] + p + 1)
                    for t in (2 * p, 2 * p + 1):
                        stt(X[:, t, :], Z[:, t, :], col(gain, t), X[:, t, :], ALU.mult, ALU.add).then_inc(x_ready, 1)
                    if p > 0:
                        dve.wait_ge(x_ready, x0 + 2 * p)
                        pair_lo(X, p - 1, v)
                dve.wait_ge(x_ready, x0 + 8)
                pair_lo(X, 3, v)

            def out_loop(b0, ada0):
                with dve.Fori(0, 4) as i:
                    for j in range(4):
                        split(b0 + j, 1024, 4, i)
                        if j == 3:
                            ada(ada0, 0, 0, 2, i)
                    ada(ada0 + 1, 1, 0, 2, i)

            def ple_update(bg, ag, x0, g0):
                def update(f, i):
                    dve.wait_ge(act_free, ag + f + 3 + 2 * i)
                    sg = SGT[:, f, :].rearrange("p (a t) -> p a t", a=2)
                    tt(sg, sg, dyn(PP, 4 * i + 2 * f, 2), ALU.mult).then_inc(gate_t, 1)
                    dve.wait_ge(gate_t, g0 + 2 * i + f + 1)
                    x = dyn(X, 4 * i + 2 * f, 2)
                    tt(x, x, sg, ALU.add).then_inc(x_ready, 1)

                with dve.Fori(0, 2) as i:
                    for j in range(4):
                        split(bg + j, 1024, 4, i)
                        if j == 2:
                            update(0, i)
                    update(1, i)

            def p_lo(layer):
                dve.wait_ge(ph_ready, layer + 1)
                tt(Sl[:, 0:2, :], praw[:], f32(Sh[:, 0:2, :]), ALU.subtract).then_inc(p_ready, 1)

            nc.vector.memset(prime[:, 0:1], 0.0).then_inc(pe_done, RING)
            nc.vector.memset(prime[:, 1:2], 0.0).then_inc(lo_done, RING)
            nc.vector.memset(prime[:, 2:3], 0.0).then_inc(act_free, 2)
            nc.vector.memset(prime[:, 3:4], 0.0).then_inc(dve_free, 2)
            nc.vector.memset(prime[:, 4:5], 0.0).then_inc(ada_used, 2)
            nc.vector.memset(prime[:, 5:6], 0.0).then_inc(o_free, 1)
            nc.vector.memset(prime[:, 6:7], 0.0).then_inc(groot, 1)
            nc.vector.memset(prime[:, 7:8], 0.0).then_inc(mo_gated, 1)
            nc.vector.memset(ones[:], 1.0).then_inc(const_ready, 1)
            nc.vector.memset(ada_acc[:], 0.0).then_inc(ada_zero, 1)
            dve.wait_ge(ada_zero, 1)
            dve.wait_ge(in_cols, 16)
            dve.wait_ge(in_pos, 16)
            step = [0]

            def chained(op):
                step[0] += 1
                op.then_inc(trig_step, 1)
                dve.wait_ge(trig_step, step[0])

            chained(nc.vector.tensor_copy(posf, posi))
            chained(ts(rt, over(posf, 2), col("invf_ret"), None, ALU.mult))
            chained(ts(rk[:, 0, :], rt[:, 0, :], 1.0 / TWO_PI, 0.25, ALU.mult, ALU.add))
            chained(ts(rk[:, 1, :], rt[:, 1, :], 1.0 / TWO_PI, None, ALU.mult))
            chained(ts(rk, rk, ROUND, None, ALU.add))
            chained(ts(rk, rk, ROUND, None, ALU.subtract))
            for c in TURN:
                chained(stt(rt, rk, -c, rt, ALU.mult, ALU.add))
            chained(ts(rt[:, 0, :], rt[:, 0, :], float(np.float32(np.pi / 2)), None, ALU.add))
            ts(rt, rt, PI_IN, -PI_IN, ALU.min, ALU.max).then_inc(trig_arg, 1)
            split(-3)
            pre_norm(S_PRE0, H_RET, "pre0")
            split(-2)
            split(-1)
            p_lo(0)
            dve.wait_ge(trig_ready, 1)
            dve.wait_ge(in_const, 16 * 4)
            dve.wait_ge(silu_c, 1)

            with dve.Fori(0, RET_HEADS) as i:
                def gated(t, b):
                    return stt(YF[:, t, :], b[:, T * (t % 2):T * (t % 2) + T], dcol("gn", 4 * i + t), SG[:, t, :],
                               ALU.mult, ALU.mult)

                for j in range(12):
                    split(B_HEAD + j, 1024, 12, i)
                    if j == 2:
                        used(B_HEAD + 1, 12, i)
                        rope(GD[0], TA, TB, 0, Q, 1, dve_free, V_HEAD + 3, rope_ready, 2, (2, 2, 4), i)
                    if j == 4:
                        used(B_HEAD + 3, 12, i)
                        rope(GD[1], TA, TB, 0, K, 2, dve_free, V_HEAD + 4, rope_ready, 4, (2, 2, 4), i)
                    if j == 3:
                        ada(0, 0, 0, 4, i)
                    if j == 5:
                        ada(1, 1, 0, 4, i)
                    if j == 8:
                        dve.wait_ge(at_ready, i + 1)
                        m = maskd[:, bass.ds(i, 1), :].rearrange("p a t -> p (a t)")
                        tt(AT[:, 0:T], M2[:, 0:T], m, ALU.mult).then_inc(atm_ready, 1)
                        tt(AT[:, T:T + P], M2[:, T:T + P], m[:, 0:P], ALU.mult).then_inc(atm_ready, 1)
                        ada(2, 0, 1, 4, i)
                    if j == 9:
                        ada(3, 1, 1, 4, i)
                    if j == 10:
                        dve.wait_ge(act_free, A_HEAD + 3 + 2 * i)
                        dve.wait_ge(gsq, 2 * i + 1)
                        gated(0, M3)
                        gated(1, M3)
                dve.wait_ge(act_free, A_HEAD + 4 + 2 * i)
                dve.wait_ge(gsq, 2 * i + 2)
                gated(2, M2)
                gated(3, M2).then_inc(o_free, 1)
                dve.wait_ge(groot, i + 2)
                nc.vector.reciprocal(rstd[:], root[:]).then_inc(grs, 1)
                dve.wait_ge(grs, i + 1)
                dve.wait_ge(o_free, i + 2)
                tt(YF, YF, over(rstd[:], 4), ALU.mult).then_inc(yf_ready, 1)
                dve.wait_ge(yh_ready, i + 1)
                tt(dyn(Yl, 4 * i, 4), YF, f32(dyn(Yh, 4 * i, 4)), ALU.subtract).then_inc(y_ready, 1)
            mod_read(0, 0, 2)
            out_loop(B_RO, 16)
            split(B_PJ0)
            split(B_PJ0 + 1)
            post_norm(S_POST0, H_PLE0, "post0", A_PJ0 + 2, X_POST0)
            mod_read(1, 2, 1)
            dve.wait_ge(act_free, A_PG0 + 2)
            ple_update(B_PG0, A_PG0, X_PLE0, 0)

            dve.wait_ge(x_ready, X_POST1)
            pre_norm(S_PRE1, H_MLA, "pre1")
            with dve.Fori(0, 2) as i:
                for j in range(4):
                    split(B_MIN + j, 1024, 4, i)
            split(B_MIN + 8)
            split(B_MIN + 9)
            p_lo(1)
            for s, p0, p1 in ((S_Q, 0, 3), (S_KV, 3, 4)):
                rstd_of(s)
                for p in range(p0, p1):
                    tt(pair(Z, p), pair(Z, p), over(rstd[:], 2), ALU.mult).then_inc(t_ready, 1)
            dve.wait_ge(t_ready, T_BEFORE[S_KV] + 1)
            for t in range(8):
                dve.wait_ge(cqh_ready, t + 1)
                h, l, t0, g = (Yh, Yl, 16 + t, col("qn", t)) if t < 6 else (Sh, Sl, t - 4, col("kvn", t - 6))
                stt(l[:, t0, :], Z[:, t, :], g, f32(h[:, t0, :]), ALU.mult, ALU.subtract).then_inc(cq_ready, 1)
            used(B_MIN + 9)
            dve.wait_ge(trig_ready, 2)
            rope(GD[0], TC[:, 0, :].rearrange("p (a t) -> p a t", a=2), TC[:, 1, :].rearrange("p (a t) -> p a t", a=2),
                 2, KR, 2 * RET_HEADS + 1, dve_free, V_KR + 4, qr_ready, 2, frees=2)
            for j in range(4):
                split(B_MG + j)

            def group(o, i, gates):
                base = B_GRP + 12 * o

                def at(n, per):
                    return n + per * o + per * i

                def masked(h):
                    dve.wait_ge(s_psum, at(h + 1, 4))
                    if h >= 2:
                        dve.wait_ge(t_psum, at(h - 1, 4))
                    s = h % 2
                    tt(SM[:, s, :], GD[s][:, 0:P + T], tri[:], ALU.add).then_inc(s_masked, 1)
                    dve.wait_ge(s_masked, at(h + 1, 4))
                    nc.vector.reduce_max(small[:, s, 0:1], SM[:, s, 0:P], AX_X).then_inc(s_max, 1)
                    nc.vector.reduce_max(small[:, s, 1:2], SM[:, s, P:P + T], AX_X).then_inc(s_max, 1)
                    dve.wait_ge(s_max, at(2 * h + 2, 8))
                    ts(small[:, s, 2:4], small[:, s, 0:2], -SCALE, None, ALU.mult).then_inc(s_bias, 1)

                def normed(h):
                    dve.wait_ge(s_exp, at(2 * h + 2, 8))
                    s = h % 2
                    nc.vector.reciprocal(small[:, s, 6:8], small[:, s, 4:6]).then_inc(s_inv, 1)
                    dve.wait_ge(s_inv, at(h + 1, 4))
                    ts(SM[:, s, 0:P], SM[:, s, 0:P], small[:, s, 6:7], None, ALU.mult).then_inc(s_prob, 1)
                    ts(SM[:, s, P:P + T], SM[:, s, P:P + T], small[:, s, 7:8], None, ALU.mult).then_inc(s_prob, 1)

                def gate_head(h):
                    dve.wait_ge(mo_psum, at(h + 1, 4))
                    tt(YG[:, h:h + 1, :], (M2, M0)[h % 2][:, 0:T].unsqueeze(1), dyn(G, 4 * i + 4 * o + h, 1), ALU.mult)\
                        .then_inc(mo_gated, 1)

                for j in range(12 if gates else 8):
                    split(base + j, 768 if j < 5 else 1024, 12, i)
                    if j == 2:
                        ada(24 + 4 * o, 0, 0, 4, i, o)
                    if j == 3:
                        ada(25 + 4 * o, 1, 0, 4, i, o)
                    if j == 4:
                        used(base + 3, 12, i)
                        rope(M2, TC[:, 0, :].rearrange("p (a t) -> p a t", a=2),
                             TC[:, 1, :].rearrange("p (a t) -> p a t", a=2), 2, QR, 2 * RET_HEADS + 2 + o, rope_read, 1 + o,
                             qr_ready, 4 + 2 * o, (1, 1, 2), i)
                    if j == 6:
                        ada(26 + 4 * o, 0, 1, 4, i, o)
                    if j == 7:
                        ada(27 + 4 * o, 1, 1, 4, i, o)
                        if gates:
                            masked(0)
                            masked(1)
                    if j == 8:
                        normed(0)
                        normed(1)
                    if j == 9:
                        masked(2)
                        masked(3)
                    if j == 10:
                        normed(2)
                        normed(3)
                    if j == 11:
                        gate_head(0)
                        gate_head(1)
                if not gates:
                    for h in (0, 2):
                        masked(h)
                        masked(h + 1)
                        if h == 2:
                            gate_head(0)
                            gate_head(1)
                        normed(h)
                        normed(h + 1)
                gate_head(2)
                gate_head(3)
                dve.wait_ge(mo_gated, at(5, 4))
                dve.wait_ge(yh_ready, RET_HEADS + o + i + 1)
                tt(dyn(Yl, 4 * i + 4 * o, 4), YG, f32(dyn(Yh, 4 * i + 4 * o, 4)), ALU.subtract).then_inc(y_ready, 1)

            with dve.Fori(0, 3) as i:
                group(0, i, True)
            group(3, 0, False)
            mod_read(2, 3, 2)
            out_loop(B_MO, 40)
            for g in (1, 4):
                ts(mod[:, 8 * g:8 * g + 8], mod[:, 8 * g:8 * g + 8], 1.0, None, ALU.add).then_inc(mod_one, 1)
            split(B_PJ1)
            split(B_PJ1 + 1)
            post_norm(S_POST1, H_PLE1, "post1", A_PJ1 + 2, X_POST1)
            mod_read(3, 5, 1)
            dve.wait_ge(act_free, A_PG1 + 2)
            ple_update(B_PG1, A_PG1, X_PLE1, 4)

            def layer_norm(s, src, n, between=None):
                k = LN_INDEX[s]
                c0 = sum(LN_PAIRS[:k])
                dve.wait_ge(mean_psum, k + 1)
                for p in range(n // 2):
                    stt(pair(Z, p), over(M2[:, 0:T], 2), -1.0 / (n * P), pair(src, p), ALU.mult, ALU.add)\
                        .then_inc(centred, 1)
                dve.wait_ge(centred, c0 + n // 2)
                if between is not None:
                    between()
                rstd_of(s)
                for p in range(n // 2):
                    tt(pair(Z, p), pair(Z, p), over(rstd[:], 2), ALU.mult).then_inc(t_ready, 1)

            dve.wait_ge(x_ready, X_DONE)
            dve.wait_ge(mod_one, 2)
            layer_norm(S_LNA, X, 8)
            nc.vector.memset(CI[:, :, 0:30], 0.0).then_inc(ci_pad, 1)
            for p in range(4):
                pair_lo(Z, p, H_CONV)
            dve.wait_ge(ci_pad, 1)
            with dve.Fori(0, 2) as i:
                def gated_value(f, i):
                    dve.wait_ge(sgt_ready, 2 * i + f + 1)
                    tt(CI[:, bass.ds(2 * i + f, 1), 30:30 + T], GD[f][:, 0:T].unsqueeze(1), SGT[:, f:f + 1, 0:T],
                       ALU.mult).then_inc(dve_free, 1)

                for j in range(4):
                    split(B_WA + j, 1024, 4, i)
                    if j == 2:
                        gated_value(0, i)
                gated_value(1, i)
            dve.wait_ge(dve_free, V_WA + 4 + 2)
            def taps(k, i=0, per=0):
                for c in range(3):
                    x = CI[:, c, bass.ds(k + per * i, T)]
                    w_tap = dcol("dwa", CONV_K * c + k + per * i)
                    if per == 0 and k == 0:
                        ts(CO[:, c, :], x, w_tap, col("bdwa", c), ALU.mult, ALU.add).then_inc(conv_step, 1)
                    else:
                        dve.wait_ge(conv_step, 3 * k + c - 2 + 3 * per * i)
                        stt(CO[:, c, :], x, w_tap, CO[:, c, :], ALU.mult, ALU.add).then_inc(conv_step, 1)

            for j in range(4):
                split(B_WP + j)
                for k in ((0, 1), (2, 3), (4, 5), (6,))[j]:
                    taps(k)
            with dve.Fori(0, 4) as i:
                for j in range(4):
                    split(B_WG + j, 1024, 4, i)
                    for k in ((7, 8), (9,), (10, 11), (12,))[j]:
                        taps(k, i, 6)
            def pooled_lo():
                dve.wait_ge(pooled_hi, 1)
                tt(Sl[:], PO, f32(Sh[:]), ALU.subtract).then_inc(pooled_ready, 1)
                split(B_POOL)

            dve.wait_ge(conv_step, 3 * CONV_K)
            dve.wait_ge(conv_sum, CONV_K)

            def pool_branch(tiles):
                used(B_POOL)
                dve.wait_ge(act_free, A_UP + 2)
                for n in tiles:
                    op = stt(G[:, 8 + n, :], bank[2 + n // 2][:, T * (n % 2):T * (n % 2) + T], col("ps", n),
                             G[:, 8 + n, :], ALU.mult, ALU.mult)
                    if n % 2 == 1:
                        op.then_inc(dve_free, 1)

            layer_norm(S_CONV, CO, 4, pooled_lo)
            pool_branch(range(4))
            for p in range(2):
                dve.wait_ge(convh_ready, p + 1)
                tt(pair(Yl, p), pair(Z, p), f32(pair(Yh, p)), ALU.subtract).then_inc(conv_ready, 1)
            pool_branch(range(4, 8))
            for j in range(6):
                if j < 4:
                    split(B_PW + j)
                if j == 1:
                    ts(X[:], X[:], ALPHA, None, ALU.mult).then_inc(xs_ready, 1)
                if 1 <= j < 5:
                    p = j - 1
                    used(B_PW + p)
                    tt(pair(Z, p), wide(GD[(V_PW + p) % 2]), pair(G, p), ALU.mult).then_inc(dve_free, 1)
                    dve.wait_ge(dve_free, V_PW + p + 3)
                    tt(pair(Z, p), pair(Z, p), pair(G, 4 + p), ALU.add).then_inc(merged_t, 1)
                if j > 1:
                    dve.wait_ge(merged_t, j - 1)
                    pair_lo(Z, j - 2, H_MERGED)

            def residual(b, o, t, gate_col):
                x = dyn(X, t, 1)
                return stt(x, o.unsqueeze(1), mod[:, bass.ds(t + gate_col, 1)], x, ALU.mult, ALU.add)

            dve.wait_ge(xs_ready, 1)
            with dve.Fori(0, 2) as i:
                def mixed(f, i):
                    used(B_WO + 2 * f + 1, 4, i)
                    residual(None, GD[f][:, 0:T], 4 * i + 2 * f, 16)
                    residual(None, GD[f][:, T:2 * T], 4 * i + 2 * f + 1, 16).then_inc(dve_free, 1)

                for j in range(4):
                    split(B_WO + j, 1024, 4, i)
                    if j == 2:
                        mixed(0, i)
                mixed(1, i)
            dve.wait_ge(dve_free, V_DN + 2)
            layer_norm(S_LN1, X, 8)
            dve.wait_ge(aff, AFF[3])
            layer_norm(S_LNB, X, 8)
            for p in range(4):
                pair_lo(Z, p, H_FF)
            ts(X[:], X[:], ALPHA, None, ALU.mult).then_inc(xs_ready, 1)
            nc.vector.memset(UPAD[:, :, 0:2], 0.0).then_inc(pads, 1)
            split(B_UP)
            split(B_UP + 1)
            def hidden(n):
                dve.wait_ge(gg_ready, n)
                tt(FF, GG, CV.rearrange("p (f n) t -> p f n t", n=2)[:, :, 0, :], ALU.mult).then_inc(f_ready, 1)

            def hidden_lo(n, k):
                dve.wait_ge(fh_ready, n)
                tt(dyn(Yl, k, 2), FF, f32(dyn(Yh, k, 2)), ALU.subtract).then_inc(fl_ready, 1)

            def up_pass(o, i):
                def older_taps(f):
                    for k in (1, 0):
                        for n in range(2):
                            c = 2 * f + n
                            if k == 1:
                                dve.wait_ge(cv0, 4 * i + 4 * o + c + 1)
                                if n == 0:
                                    dve.wait_ge(act_free, A_UP + f + 3 + 2 * i + 2 * o)
                            else:
                                dve.wait_ge(cv_step, 8 * i + 8 * o + 4 * f + n + 1)
                            stt(CV[:, c, :], UPAD[:, c, k:k + T], dcol("dwf", 4 * i + 4 * o + c + 44 * k), CV[:, c, :],
                                ALU.mult, ALU.add).then_inc(cv_step, 1)

                if o:
                    hidden(i + o)
                split(B_UP + 4 * o + 2, 1024, 4, i)
                older_taps(0)
                split(B_UP + 4 * o + 3, 1024, 4, i)
                if o:
                    hidden_lo(i + o, 2 * i + 2 * o - 2)
                split(B_UP + 4 * o + 4, 1024, 4, i)
                older_taps(1)
                split(B_UP + 4 * o + 5, 1024, 4, i)

            up_pass(0, 0)
            with dve.Fori(0, 10) as i:
                up_pass(1, i)
            hidden(11)
            hidden_lo(11, FF_TILES - 2)

            def down(t, i, per):
                used(B_DN + 4 * t + 3, per, i)
                residual(None, GD[t][:, 0:T], 2 * i + t if per else 6 + t, 40).then_inc(dve_free, 1)

            dve.wait_ge(xs_ready, 2)
            with dve.Fori(0, 3) as i:
                for j in range(8):
                    split(B_DN + 2 + j, DN_TILES[(j + 1) % 4] * P, 8, i)
                    if j == 2:
                        down(0, i, 8)
                    if j == 6:
                        down(1, i, 8)
            for j in range(3):
                split(B_DN + 26 + j, DN_TILES[(j + 1) % 4] * P)
            for t in range(2):
                used(B_DN + 24 + 4 * t + 3)
                stt(X[:, 6 + t, :], GD[t][:, 0:T], mod[:, 46 + t:47 + t], X[:, 6 + t, :], ALU.mult, ALU.add)\
                    .then_inc(dve_free, 1)
            dve.wait_ge(dve_free, V_DN + 8 + 2)
            layer_norm(S_LN2, X, 8)

        @block.gpsimd
        def _(pool):
            step = [0]

            def chained(op):
                step[0] += 1
                op.then_inc(pool_step, 1)
                pool.wait_ge(pool_step, step[0])

            def angle(op):
                step[0] += 1
                op.then_inc(mla_step, 1)
                pool.wait_ge(mla_step, step[0])

            gts, gtt = nc.gpsimd.tensor_scalar, nc.gpsimd.tensor_tensor
            pool.wait_ge(in_cols, 16)
            pool.wait_ge(trig_step, 1)
            for n in range(2):
                angle(gts(mt[:, n, :], posf, col("invf_mla"), None, ALU.mult))
            angle(gts(mk[:, 0, :], mt[:, 0, :], 1.0 / TWO_PI, 0.25, ALU.mult, ALU.add))
            angle(gts(mk[:, 1, :], mt[:, 1, :], 1.0 / TWO_PI, None, ALU.mult))
            angle(gts(mk, mk, ROUND, None, ALU.add))
            angle(gts(mk, mk, ROUND, None, ALU.subtract))
            for c in TURN:
                angle(gts(mp, mk, -c, None, ALU.mult))
                angle(gtt(mt, mt, mp, ALU.add))
            angle(gts(mt[:, 0, :], mt[:, 0, :], float(np.float32(np.pi / 2)), None, ALU.add))
            gts(mt, mt, PI_IN, -PI_IN, ALU.min, ALU.max).then_inc(mla_arg, 1)
            step[0] = 0
            pool.wait_ge(dve_free, V_WA + 3)
            nc.gpsimd.memset(U[:, :, 0:16], 0.0).then_inc(pads, 1)
            pool.wait_ge(pads, 1)

            def add_tap(k, i=0, per=0):
                pool.wait_ge(tap_ready, k + 1 + per * i)
                pool.wait_ge(conv_sum, k + per * i)
                gtt(CO[:, 3, :], CO[:, 3, :], TP[:, k % 3, :], ALU.add).then_inc(conv_sum, 1)

            pool.wait_ge(tap_ready, 1)
            nc.gpsimd.memset(pool_prime[:], 0.0).then_inc(conv_sum, 1)
            for k in range(1, 7):
                add_tap(k)
            pool.wait_ge(act_free, A_WP + 2 + 2)
            for g, window in enumerate(WINDOWS):
                for k in (7, 8, 9):
                    add_tap(k + 6 * g)
                src, shift, n = U[:, g, :], 1, 0
                while shift < window:
                    lo = 2 * shift - 1
                    dst = W1[:, n % 2, :]
                    chained(gtt(dst[:, lo:16 + T], src[:, lo:16 + T], src[:, lo - shift:16 + T - shift], ALU.add))
                    src, shift, n = dst, 2 * shift, n + 1
                chained(gtt(src[:, 16:32], src[:, 16:32], cnt[:, g, :], ALU.mult))
                chained(gts(src[:, 16:16 + T], src[:, 16:16 + T], 1.0 / window, None, ALU.mult))
                gtt(PO[:, g, :], src[:, 16:16 + T], U[:, g, 16:16 + T], ALU.subtract).then_inc(pooled, 1)
                pool.wait_ge(pooled, g + 1)
                for k in (10, 11, 12):
                    add_tap(k + 6 * g)


def _features(a):
    return np.ascontiguousarray(a.T.reshape(-1, P, a.shape[0]).transpose(1, 0, 2))


def _tiles(a):
    return a.reshape(a.shape[0] // P, P, a.shape[1] // P, P)


def _strips(a, kts=None):
    t = _tiles(a)
    return t.transpose(2, 1, 0, 3).reshape(t.shape[2], P, -1)


def _deep(a):
    t = _strips(a)
    return t.reshape(t.shape[0], P, 2, 1024).transpose(0, 2, 1, 3).reshape(-1, P, 1024)


def _short(a, per):
    t = _strips(a)
    return t.reshape(-1, per, P, t.shape[2]).transpose(0, 2, 1, 3).reshape(-1, P, per * t.shape[2])


def _rows(a):
    return a.reshape(-1, 2, P, 512).transpose(0, 2, 1, 3).reshape(-1, P, 1024)


def _col(a):
    return a.reshape(-1, P).T


def kernel(x, p, positions, pre_norm_g, post_norm_g, ret_w_in, ret_gn_g, ret_w_out, mla_w_in, mla_q_norm_g,
           mla_kv_norm_g, mla_w_uq, mla_w_uk, mla_w_uv, mla_w_out, ple_w_proj, ple_w_gate, c_2, w_ada_2, b_ada_2,
           w_in_2, w_dw_a_2, b_dw_a_2, ln_a_g_2, ln_a_b_2, w_pw_a_2, w_pool_2, pool_scale_2, w_out_2, ln1_g_2, ln1_b_2,
           w_up_2, w_dw_f_2, b_dw_f_2, w_down_2, ln2_g_2, ln2_b_2):
    import concourse.bacc as bacc
    from concourse.bass_utils import run_bass_kernel_spmd

    f = np.float32
    cat = np.concatenate

    wi = ret_w_in[0]
    heads = []
    for h in range(RET_HEADS):
        heads += [_strips(wi[:, 256 * h:256 * h + 256]), _strips(wi[:, 1024 + 256 * h:1280 + 256 * h]),
                  _rows(wi[:, 2048 + 512 * h:2560 + 512 * h]), _strips(wi[:, 4096 + 512 * h:4608 + 512 * h])]
    mi = mla_w_in[0]
    kr = mi[:, 1024:1088]
    kr = cat([kr[:, 0:32]] * 4 + [kr[:, 32:64]] * 4, axis=1)
    uq = mla_w_uq[0].reshape(768, MLA_HEADS, MLA_NOPE + MLA_ROPE)
    uk = mla_w_uk[0].reshape(256, MLA_HEADS * MLA_NOPE)
    uv = mla_w_uv[0].reshape(256, MLA_HEADS * 128)
    uqs = []
    for g in range(4):
        hs = uq[:, 4 * g:4 * g + 4]
        uqs += [_strips(hs[:, :, 128:160].reshape(768, 128)), _strips(hs[:, :, 160:192].reshape(768, 128)),
                _strips(hs[:, :, 0:128].reshape(768, 512))]
    w2 = w_in_2[0]
    av, ag = _strips(w2[:, 0:512]), _strips(w2[:, 512:1024])
    up = _strips(w_up_2[0])
    order = [x for t in range(FF_TILES) for x in (t, FF_TILES + t)]
    down = _strips(w_down_2[0])
    downs, k0 = [], 0
    for n in DN_TILES:
        part = down[:, :, k0 * P:(k0 + n) * P]
        downs.append(cat([part, np.zeros((DT, P, (6 - n) * P), f)], axis=2) if n < 6 else part)
        k0 += n
    weights = {
        "head": cat(heads), "ret_out": _deep(ret_w_out[0]), "proj0": _short(ple_w_proj[0], 4),
        "ple_gate0": _strips(ple_w_gate[0]), "mla_qkv": _strips(mi[:, 0:1024]), "mla_kr": _strips(kr),
        "mla_gate": _strips(mi[:, 1088:]), "uk": _short(uk, 4),
        "uv": cat([_rows(uv[:, 512 * g:512 * g + 512]) for g in range(4)]), "uq": cat(uqs),
        "mla_out": _deep(mla_w_out[0]), "proj1": _short(ple_w_proj[1], 4), "ple_gate1": _strips(ple_w_gate[1]),
        "conv_in": np.stack([av, ag], axis=1).reshape(8, P, 1024), "pool_in": _strips(w2[:, 1024:1536]),
        "gates": _strips(w2[:, 1536:]),
        "pool_w": w_pool_2[0].reshape(4, P, 2, P).transpose(1, 0, 2, 3).reshape(1, P, 1024),
        "pw": _short(w_pw_a_2[0], 2), "mix": _strips(w_out_2[0]), "up": up[order],
        "down": np.stack(downs, axis=1).reshape(-1, P, 768),
    }
    ada = w_ada_2[0].reshape(8, P, 6, 1024).transpose(2, 0, 1, 3)
    ada = cat([x for g in (0, 3) for x in (ada[g:g + 2].reshape(2, 4, 2, P, 1024).transpose(1, 0, 2, 3, 4).reshape(16, P, 1024),
                                           ada[g + 2])])

    half_r, half_m = 128, 32
    inv_r = (10000.0 ** (-np.arange(half_r, dtype=np.float64) / half_r)).astype(f)
    inv_m = np.tile((10000.0 ** (-np.arange(half_m, dtype=np.float64) / half_m)).astype(f), 4)
    rel = np.arange(T)[None, :] - np.arange(P)[:, None]
    decay = [1.0 - 2.0 ** (-5.0 - h) for h in range(RET_HEADS)]
    mask = np.stack([np.where(rel >= 0, g ** np.maximum(rel, 0), 0.0) / 16.0 for g in decay], axis=1).astype(f)
    diagonal = np.where(np.arange(P)[None, :] <= np.arange(P)[:, None], 0.0, NEG).astype(f)
    tri = cat([diagonal, np.zeros((P, P), f), diagonal], axis=1)
    cnt = np.stack([n / np.minimum(np.arange(16) + 1, n) for n in WINDOWS]).astype(f)
    cnt = np.ascontiguousarray(np.broadcast_to(cnt, (P, 4, 16)))

    dwf = cat([_col(w_dw_f_2[0][k])[:, order] for k in range(3)], axis=1)
    dwa = w_dw_a_2[0].reshape(CONV_K, CONV_TILES, P).transpose(2, 1, 0).reshape(P, -1)
    cols = cat([_col(pre_norm_g[0]), _col(pre_norm_g[1]), _col(post_norm_g[0]), _col(post_norm_g[1]), _col(ret_gn_g[0]),
                _col(mla_q_norm_g[0]), _col(mla_kv_norm_g[0]), _col(b_ada_2[0]), _col(c_2[0]), dwa, _col(b_dw_a_2[0]),
                _col(ln_a_g_2[0]), _col(ln_a_b_2[0]), _col(pool_scale_2[0]), _col(ln1_g_2[0]), _col(ln1_b_2[0]), dwf,
                _col(b_dw_f_2[0])[:, order], _col(ln2_g_2[0]), _col(ln2_b_2[0]), inv_r[:, None], inv_m[:, None],
                np.full((P, 1), RMS_EPS, f), np.full((P, 1), LN_EPS, f)], axis=1)

    arrays = {
        "x_in": _features(x[0]), "p_in": np.stack([_features(p[0, 0]), _features(p[1, 0])]), "pos_in": positions[0],
        "cols_in": cols, "mask_in": mask, "tri_in": tri, "cnt_in": cnt, "ident_in": np.eye(P, dtype=f), "ada_in": ada,
    }
    arrays.update({"w_" + n: a for n, a in weights.items()})
    arrays = {n: np.ascontiguousarray(a) for n, a in arrays.items()}
    nc = bacc.Bacc("TRN2", target_bir_lowering=False, num_devices=1)
    ap = {n: nc.dram_tensor(n, a.shape, mybir.dt.from_np(a.dtype), kind="ExternalInput").ap() for n, a in arrays.items()}
    out = nc.dram_tensor("out", (P, DT, T), F32, kind="ExternalOutput").ap()
    program(nc, ap["x_in"], ap["p_in"], ap["pos_in"], ap["cols_in"], ap["mask_in"], ap["tri_in"], ap["cnt_in"],
            ap["ident_in"], ap["ada_in"], {n: ap["w_" + n] for n in weights}, out)
    got = run_bass_kernel_spmd(nc, [arrays], core_ids=[0]).results[0]["out"]
    return np.ascontiguousarray(got.transpose(1, 0, 2).reshape(D, T).T)[None]
```
